# Optimizing a Trainium2 kernel written in Bass

```python
import math
import jax
import jax.numpy as jnp
from jax import lax
import numpy as np

D_MODEL = 1024
BATCH = 1
SEQ = 512
DEPTH = 2

N_A_LAYERS = DEPTH // 2
N_B_LAYERS = DEPTH - N_A_LAYERS

SSM_EXPAND = 2
D_INNER = SSM_EXPAND * D_MODEL
SSM_HEAD_DIM = 64
SSM_HEADS = D_INNER // SSM_HEAD_DIM
SSM_GROUPS = 4
SSM_HEADS_PER_GROUP = SSM_HEADS // SSM_GROUPS
SSM_STATE = 128
SSM_CONV = 4
SSM_CHUNK = 128
SSM_CONV_DIM = D_INNER + 2 * SSM_GROUPS * SSM_STATE
SSM_IN_DIM = D_INNER + SSM_CONV_DIM + SSM_HEADS

ATT_HEAD_DIM = 64
ATT_HEADS = D_MODEL // (2 * ATT_HEAD_DIM)
ATT_V_DIM = 2 * ATT_HEAD_DIM
ATT_BLOCK = 128
K_DIM = ATT_HEADS * 2 * ATT_HEAD_DIM
V_TOTAL = ATT_HEADS * ATT_V_DIM

NUM_BUCKETS = 32
MAX_DISTANCE = 128

FFN_DIM = 256 * ((8 * D_MODEL // 3 + 255) // 256)
FFN_CONV = 3

EPS = 1e-6


def rms_norm(x, g):
    xf = x.astype(jnp.float32)
    y = xf * lax.rsqrt(jnp.mean(xf * xf, axis=-1, keepdims=True) + EPS)
    return y.astype(x.dtype) * g

def causal_dwconv(u, w, b):
    k_w = w.shape[0]
    s = u.shape[1]
    up = jnp.pad(u, ((0, 0), (k_w - 1, 0), (0, 0)))
    y = up[:, 0:s] * w[0]
    for k in range(1, k_w):
        y = y + up[:, k:k + s] * w[k]
    return y + b

def segsum(a):
    t = a.shape[-1]
    cs = jnp.cumsum(a, axis=-1)
    d = cs[..., :, None] - cs[..., None, :]
    mask = jnp.tril(jnp.ones((t, t), dtype=bool))
    return jnp.where(mask, d, -jnp.inf)

def ssd_chunked(xdt, a, bm, cm):
    b, s, h, p = xdt.shape
    g, r, l = SSM_GROUPS, SSM_HEADS_PER_GROUP, SSM_CHUNK
    c = s // l
    xc = xdt.reshape(b, c, l, g, r, p)
    ac = a.reshape(b, c, l, g, r).transpose(0, 3, 4, 1, 2)
    bc = bm.reshape(b, c, l, g, SSM_STATE)
    cc = cm.reshape(b, c, l, g, SSM_STATE)
    a_cs = jnp.cumsum(ac, axis=-1)
    decay_in = jnp.exp(segsum(ac))
    cb = jnp.einsum('bclgn,bcsgn->bcgls', cc, bc)
    y_diag = jnp.einsum('bcgls,bgrcls,bcsgrp->bclgrp', cb, decay_in, xc)
    decay_states = jnp.exp(a_cs[..., -1:] - a_cs)
    states = jnp.einsum('bclgn,bgrcl,bclgrp->bcgrpn', bc, decay_states, xc)
    states0 = jnp.concatenate([jnp.zeros_like(states[:, :1]), states], axis=1)
    chunk_tot = jnp.pad(a_cs[..., -1], ((0, 0), (0, 0), (0, 0), (1, 0)))
    decay_chunk = jnp.exp(segsum(chunk_tot))
    new_states = jnp.einsum('bgrzc,bcgrpn->bzgrpn', decay_chunk, states0)
    states_in = new_states[:, :-1]
    y_off = jnp.einsum('bclgn,bcgrpn,bgrcl->bclgrp', cc, states_in, jnp.exp(a_cs))
    return (y_diag + y_off).reshape(b, s, h, p)

def mamba2_mixer(x, ln_g, in_w, conv_w, conv_b, dt_bias, a_log, d_skip, norm_g, out_w):
    b, s, _ = x.shape
    zxbcdt = rms_norm(x, ln_g) @ in_w
    z = zxbcdt[..., :D_INNER]
    xbc = zxbcdt[..., D_INNER:D_INNER + SSM_CONV_DIM]
    dt = zxbcdt[..., D_INNER + SSM_CONV_DIM:]
    xbc = jax.nn.silu(causal_dwconv(xbc, conv_w, conv_b))
    gn = SSM_GROUPS * SSM_STATE
    xs = xbc[..., :D_INNER].reshape(b, s, SSM_HEADS, SSM_HEAD_DIM)
    bm = xbc[..., D_INNER:D_INNER + gn].reshape(b, s, SSM_GROUPS, SSM_STATE)
    cm = xbc[..., D_INNER + gn:].reshape(b, s, SSM_GROUPS, SSM_STATE)
    dt = jax.nn.softplus(dt.astype(jnp.float32) + dt_bias.astype(jnp.float32))
    a = dt * (-jnp.exp(a_log.astype(jnp.float32)))
    xs32 = xs.astype(jnp.float32)
    y = ssd_chunked(xs32 * dt[..., None], a, bm.astype(jnp.float32), cm.astype(jnp.float32))
    y = y + xs32 * d_skip.astype(jnp.float32)[:, None]
    y = y.reshape(b, s, D_INNER) * jax.nn.silu(z.astype(jnp.float32))
    y = rms_norm(y.reshape(b, s, SSM_GROUPS, D_INNER // SSM_GROUPS),
                 norm_g.reshape(SSM_GROUPS, D_INNER // SSM_GROUPS)).reshape(b, s, D_INNER)
    return y @ out_w

def conv_ffn(x, ln_g, up_w, conv_w, conv_b, down_w):
    u = causal_dwconv(rms_norm(x, ln_g) @ up_w, conv_w, conv_b)
    gate, up = u[..., :FFN_DIM], u[..., FFN_DIM:]
    return (jax.nn.silu(gate) * up) @ down_w

def shared_kv(x, kv_ln_g, kv_w, k_norm_g):
    b, s, _ = x.shape
    kv = rms_norm(x, kv_ln_g) @ kv_w
    k = kv[..., :K_DIM].reshape(b, s, ATT_HEADS, 2, ATT_HEAD_DIM)
    v = kv[..., K_DIM:].reshape(b, s, ATT_HEADS, ATT_V_DIM)
    return rms_norm(k, k_norm_g), v

def t5_bucket(dist):
    n = jnp.maximum(dist, 0)
    max_exact = NUM_BUCKETS // 2
    nf = jnp.maximum(n, 1).astype(jnp.float32)
    large = max_exact + (jnp.log(nf / max_exact) / math.log(MAX_DISTANCE / max_exact)
                         * (NUM_BUCKETS - max_exact)).astype(jnp.int32)
    large = jnp.minimum(large, NUM_BUCKETS - 1)
    return jnp.where(n < max_exact, n, large)

def diff_attention(x, k, v, rel_bias, ln_g, q_w, q_norm_g, lam_vecs, subln_g, out_w, lam_init):
    b, s, _ = x.shape
    q = (rms_norm(x, ln_g) @ q_w).reshape(b, s, ATT_HEADS, 2, ATT_HEAD_DIM)
    q = rms_norm(q, q_norm_g)
    lv = lam_vecs.astype(jnp.float32)
    lam = jnp.exp(jnp.sum(lv[0] * lv[1])) - jnp.exp(jnp.sum(lv[2] * lv[3])) + lam_init
    scale = ATT_HEAD_DIM ** -0.5
    nb = s // ATT_BLOCK
    qb = q.reshape(b, nb, ATT_BLOCK, ATT_HEADS, 2, ATT_HEAD_DIM).transpose(1, 0, 2, 3, 4, 5)
    kpos = jnp.arange(s)

    def block(args):
        qblk, i = args
        qpos = i * ATT_BLOCK + jnp.arange(ATT_BLOCK)
        dist = qpos[:, None] - kpos[None, :]
        bias = rel_bias[t5_bucket(dist)].astype(jnp.float32).transpose(2, 0, 1)
        logits = jnp.einsum('bqhcd,bkhcd->bhcqk', qblk, k).astype(jnp.float32) * scale
        logits = logits + bias[None, :, None]
        logits = jnp.where(dist >= 0, logits, -jnp.inf)
        p = jax.nn.softmax(logits, axis=-1)
        attn = p[:, :, 0] - lam * p[:, :, 1]
        return jnp.einsum('bhqk,bkhd->bqhd', attn.astype(v.dtype), v)

    o = lax.map(block, (qb, jnp.arange(nb)))
    o = o.transpose(1, 0, 2, 3, 4).reshape(b, s, ATT_HEADS, ATT_V_DIM)
    o = rms_norm(o, subln_g) * (1.0 - lam_init)
    return o.reshape(b, s, V_TOTAL) @ out_w

def first_inputs(seed: int = 0) -> dict:
    key = jax.random.key(seed)
    ks = jax.random.split(key, 32)
    f32 = jnp.float32

    def nrm(k, shape, scale):
        return jax.random.normal(k, shape, f32) * scale

    def gain(k, shape):
        return 1.0 + 0.02 * jax.random.normal(k, shape, f32)

    na, nb = N_A_LAYERS, N_B_LAYERS
    dt = jnp.exp(jax.random.uniform(ks[6], (na, SSM_HEADS), f32)
                 * (math.log(0.1) - math.log(0.001)) + math.log(0.001))
    return {
        'x': nrm(ks[0], (BATCH, SEQ, D_MODEL), 1.0),
        'ssm_ln_g': gain(ks[1], (na, D_MODEL)),
        'ssm_in_w': nrm(ks[2], (na, D_MODEL, SSM_IN_DIM), D_MODEL ** -0.5),
        'ssm_conv_w': nrm(ks[3], (na, SSM_CONV, SSM_CONV_DIM), SSM_CONV ** -0.5),
        'ssm_conv_b': nrm(ks[4], (na, SSM_CONV_DIM), 0.02),
        'ssm_dt_bias': dt + jnp.log(-jnp.expm1(-dt)),
        'ssm_a_log': jnp.log(jax.random.uniform(ks[7], (na, SSM_HEADS), f32, 1.0, 16.0)),
        'ssm_d': gain(ks[8], (na, SSM_HEADS)),
        'ssm_norm_g': gain(ks[9], (na, D_INNER)),
        'ssm_out_w': nrm(ks[10], (na, D_INNER, D_MODEL), D_INNER ** -0.5),
        'kv_ln_g': gain(ks[11], (D_MODEL,)),
        'kv_w': nrm(ks[12], (D_MODEL, K_DIM + V_TOTAL), D_MODEL ** -0.5),
        'k_norm_g': gain(ks[13], (ATT_HEAD_DIM,)),
        'rel_bias': nrm(ks[14], (NUM_BUCKETS, ATT_HEADS), 0.5),
        'attn_ln_g': gain(ks[15], (nb, D_MODEL)),
        'q_w': nrm(ks[16], (nb, D_MODEL, K_DIM), D_MODEL ** -0.5),
        'q_norm_g': gain(ks[17], (nb, ATT_HEAD_DIM)),
        'lam_vecs': nrm(ks[18], (nb, 4, ATT_HEAD_DIM), 0.1),
        'subln_g': gain(ks[19], (nb, ATT_V_DIM)),
        'attn_out_w': nrm(ks[20], (nb, V_TOTAL, D_MODEL), V_TOTAL ** -0.5),
        'ffn_ln_g': gain(ks[21], (DEPTH, D_MODEL)),
        'ffn_up_w': nrm(ks[22], (DEPTH, D_MODEL, 2 * FFN_DIM), D_MODEL ** -0.5),
        'ffn_conv_w': nrm(ks[23], (DEPTH, FFN_CONV, 2 * FFN_DIM), FFN_CONV ** -0.5),
        'ffn_conv_b': nrm(ks[24], (DEPTH, 2 * FFN_DIM), 0.02),
        'ffn_down_w': nrm(ks[25], (DEPTH, FFN_DIM, D_MODEL), FFN_DIM ** -0.5),
    }

def first_block(x, ssm_ln_g, ssm_in_w, ssm_conv_w, ssm_conv_b, ssm_dt_bias, ssm_a_log, ssm_d,
              ssm_norm_g, ssm_out_w, kv_ln_g, kv_w, k_norm_g, rel_bias, attn_ln_g, q_w,
              q_norm_g, lam_vecs, subln_g, attn_out_w, ffn_ln_g, ffn_up_w, ffn_conv_w,
              ffn_conv_b, ffn_down_w):
    k_sh, v_sh = None, None
    for layer in range(DEPTH):
        if layer < N_A_LAYERS:
            i = layer
            mix = mamba2_mixer(x, ssm_ln_g[i], ssm_in_w[i], ssm_conv_w[i], ssm_conv_b[i],
                               ssm_dt_bias[i], ssm_a_log[i], ssm_d[i], ssm_norm_g[i],
                               ssm_out_w[i])
        else:
            j = layer - N_A_LAYERS
            if j == 0:
                k_sh, v_sh = shared_kv(x, kv_ln_g, kv_w, k_norm_g)
            lam_init = 0.8 - 0.6 * math.exp(-0.3 * layer)
            mix = diff_attention(x, k_sh, v_sh, rel_bias, attn_ln_g[j], q_w[j], q_norm_g[j],
                                 lam_vecs[j], subln_g[j], attn_out_w[j], lam_init)
        x = x + mix.astype(x.dtype)
        ff = conv_ffn(x, ffn_ln_g[layer], ffn_up_w[layer], ffn_conv_w[layer],
                      ffn_conv_b[layer], ffn_down_w[layer])
        x = x + ff.astype(x.dtype)
    return x


DEPTH_2 = 1

HEAD_DIM = 64
BRANCH_WIDTH = D_MODEL // 2
N_BRANCH = 3
CONV_WIDTH = BRANCH_WIDTH
CONV_K = 3
FOX_HEADS = BRANCH_WIDTH // HEAD_DIM
SWA_HEADS = BRANCH_WIDTH // HEAD_DIM
SWA_KV_HEADS = 2
SWA_GROUP = SWA_HEADS // SWA_KV_HEADS
WINDOW = 128
BLOCK = 128
N_BUCKETS = 32
MAX_DISTANCE_2 = WINDOW
MEM_LEN = 256
X_HEADS = 4
X_HEAD_DIM = D_MODEL // X_HEADS
_FF_RAW = -(-8 * D_MODEL // 3)
D_FF = -(-_FF_RAW // 256) * 256
IN_COLS = (3 * CONV_WIDTH + 3 * FOX_HEADS * HEAD_DIM + FOX_HEADS
           + (SWA_HEADS + 2 * SWA_KV_HEADS) * HEAD_DIM + N_BRANCH * D_MODEL)
RMS_EPS = 1e-6
NEG_INF = -1e30


def rms_norm_2(x, g):
    xf = x.astype(jnp.float32)
    y = xf * lax.rsqrt(jnp.mean(xf * xf, axis=-1, keepdims=True) + RMS_EPS)
    return (y * g.astype(jnp.float32)).astype(x.dtype)

def split_proj(proj):
    sizes = ([CONV_WIDTH] * 3 + [FOX_HEADS * HEAD_DIM] * 3 + [FOX_HEADS]
             + [SWA_HEADS * HEAD_DIM, SWA_KV_HEADS * HEAD_DIM, SWA_KV_HEADS * HEAD_DIM]
             + [N_BRANCH * D_MODEL])
    parts, off = [], 0
    for s in sizes:
        parts.append(proj[..., off:off + s])
        off += s
    return parts

def short_conv_branch(gate_b, gate_c, u, conv_w):
    z = gate_c * u
    y = lax.conv_general_dilated(
        z, conv_w[:, None, :].astype(z.dtype), window_strides=(1,),
        padding=[(CONV_K - 1, 0)], dimension_numbers=('NWC', 'WIO', 'NWC'),
        feature_group_count=CONV_WIDTH)
    return gate_b * y

def fox_branch(q, k, v, f_logit, f_bias):
    b, s = q.shape[0], q.shape[1]
    nb = s // BLOCK
    q = q.reshape(b, s, FOX_HEADS, HEAD_DIM)
    k = k.reshape(b, s, FOX_HEADS, HEAD_DIM)
    v = v.reshape(b, s, FOX_HEADS, HEAD_DIM)
    log_f = jax.nn.log_sigmoid(f_logit.astype(jnp.float32) + f_bias.astype(jnp.float32))
    c = jnp.cumsum(log_f, axis=1)
    c_k = c.transpose(0, 2, 1)
    q_blocks = q.reshape(b, nb, BLOCK, FOX_HEADS, HEAD_DIM).transpose(1, 0, 2, 3, 4)
    c_blocks = c.reshape(b, nb, BLOCK, FOX_HEADS).transpose(1, 0, 2, 3)
    starts = jnp.arange(nb, dtype=jnp.int32) * BLOCK
    k_pos = jnp.arange(s, dtype=jnp.int32)
    scale = HEAD_DIM ** -0.5

    def one_block(args):
        qi, ci, start = args
        logits = jnp.einsum('bqhd,bkhd->bhqk', qi, k).astype(jnp.float32) * scale
        logits = logits + ci.transpose(0, 2, 1)[..., None] - c_k[:, :, None, :]
        q_pos = start + jnp.arange(BLOCK, dtype=jnp.int32)
        causal = k_pos[None, :] <= q_pos[:, None]
        logits = jnp.where(causal[None, None], logits, NEG_INF)
        p = jax.nn.softmax(logits, axis=-1)
        return jnp.einsum('bhqk,bkhd->bqhd', p.astype(v.dtype), v)

    out = lax.map(one_block, (q_blocks, c_blocks, starts))
    return out.transpose(1, 0, 2, 3, 4).reshape(b, s, FOX_HEADS * HEAD_DIM)

def t5_bucket_2(n):
    n = jnp.maximum(n, 0)
    max_exact = N_BUCKETS // 2
    large = max_exact + (
        jnp.log(jnp.maximum(n, 1).astype(jnp.float32) / max_exact)
        / math.log(MAX_DISTANCE_2 / max_exact) * (N_BUCKETS - max_exact)).astype(jnp.int32)
    large = jnp.minimum(large, N_BUCKETS - 1)
    return jnp.where(n < max_exact, n, large)

def swa_sink_branch(q, k, v, rel_bias, sink):
    b, s = q.shape[0], q.shape[1]
    nb = s // BLOCK
    qb = q.reshape(b, nb, BLOCK, SWA_KV_HEADS, SWA_GROUP, HEAD_DIM)
    kb = k.reshape(b, nb, BLOCK, SWA_KV_HEADS, HEAD_DIM)
    vb = v.reshape(b, nb, BLOCK, SWA_KV_HEADS, HEAD_DIM)

    def band(t):
        prev = jnp.concatenate([jnp.zeros_like(t[:, :1]), t[:, :-1]], axis=1)
        return jnp.concatenate([prev, t], axis=2)

    k_band, v_band = band(kb), band(vb)
    tq = jnp.arange(BLOCK, dtype=jnp.int32)
    sk = jnp.arange(2 * BLOCK, dtype=jnp.int32)
    dist = BLOCK + tq[:, None] - sk[None, :]
    in_window = (dist >= 0) & (dist < WINDOW)
    key_pos = jnp.arange(nb, dtype=jnp.int32)[:, None] * BLOCK - BLOCK + sk[None, :]
    mask = in_window[None] & (key_pos >= 0)[:, None, :]
    bias = rel_bias.astype(jnp.float32)[t5_bucket_2(dist)]
    bias = bias.reshape(BLOCK, 2 * BLOCK, SWA_KV_HEADS, SWA_GROUP).transpose(2, 3, 0, 1)
    logits = jnp.einsum('bnqkgd,bnskd->bnkgqs', qb, k_band).astype(jnp.float32) * HEAD_DIM ** -0.5
    logits = jnp.where(mask[None, :, None, None], logits + bias, NEG_INF)
    sink_l = sink.astype(jnp.float32).reshape(SWA_KV_HEADS, SWA_GROUP)[None, None, :, :, None]
    m = jnp.maximum(logits.max(axis=-1), sink_l)
    p = jnp.exp(logits - m[..., None])
    denom = p.sum(axis=-1) + jnp.exp(sink_l - m)
    p = p / denom[..., None]
    out = jnp.einsum('bnkgqs,bnskd->bnqkgd', p.astype(v.dtype), v_band)
    return out.reshape(b, s, SWA_HEADS * HEAD_DIM)

def cross_attention(xn, mem_n, w_q, w_kv, w_o):
    b, s = xn.shape[0], xn.shape[1]
    q = (xn @ w_q).reshape(b, s, X_HEADS, X_HEAD_DIM)
    kv = mem_n @ w_kv
    k = kv[..., :X_HEADS * X_HEAD_DIM].reshape(b, -1, X_HEADS, X_HEAD_DIM)
    v = kv[..., X_HEADS * X_HEAD_DIM:].reshape(b, -1, X_HEADS, X_HEAD_DIM)
    logits = jnp.einsum('bshd,bmhd->bhsm', q, k).astype(jnp.float32) * X_HEAD_DIM ** -0.5
    p = jax.nn.softmax(logits, axis=-1)
    o = jnp.einsum('bhsm,bmhd->bshd', p.astype(v.dtype), v).reshape(b, s, X_HEADS * X_HEAD_DIM)
    return o @ w_o

def swiglu(xn, w_gate, w_up, w_down):
    return (jax.nn.silu(xn @ w_gate) * (xn @ w_up)) @ w_down

def second_inputs(seed: int = 0) -> dict:
    key = jax.random.key(seed)
    ks = jax.random.split(key, 22)
    f32 = jnp.float32

    def nrm(k, shape, scale):
        return scale * jax.random.normal(k, shape, f32)

    def gain(k, shape):
        return 1.0 + 0.1 * jax.random.normal(k, shape, f32)

    return {
        "x": nrm(ks[0], (BATCH, SEQ, D_MODEL), 1.0),
        "mem": nrm(ks[1], (BATCH, MEM_LEN, D_MODEL), 1.0),
        "mix_norm_g": gain(ks[2], (DEPTH_2, D_MODEL)),
        "w_in": nrm(ks[3], (DEPTH_2, D_MODEL, IN_COLS), D_MODEL ** -0.5),
        "forget_bias": 4.0 + 0.5 * jax.random.normal(ks[4], (DEPTH_2, FOX_HEADS), f32),
        "conv_w": nrm(ks[5], (DEPTH_2, CONV_K, CONV_WIDTH), CONV_K ** -0.5),
        "sink": nrm(ks[6], (DEPTH_2, SWA_HEADS), 0.5),
        "w_branch": nrm(ks[7], (DEPTH_2, N_BRANCH, BRANCH_WIDTH, D_MODEL), BRANCH_WIDTH ** -0.5),
        "w_mix_out": nrm(ks[8], (DEPTH_2, D_MODEL, D_MODEL), D_MODEL ** -0.5),
        "rel_bias": nrm(ks[9], (N_BUCKETS, SWA_HEADS), 0.5),
        "xattn_norm_g": gain(ks[10], (DEPTH_2, D_MODEL)),
        "mem_norm_g": gain(ks[11], (DEPTH_2, D_MODEL)),
        "w_xq": nrm(ks[12], (DEPTH_2, D_MODEL, X_HEADS * X_HEAD_DIM), D_MODEL ** -0.5),
        "w_xkv": nrm(ks[13], (DEPTH_2, D_MODEL, 2 * X_HEADS * X_HEAD_DIM), D_MODEL ** -0.5),
        "w_xo": nrm(ks[14], (DEPTH_2, X_HEADS * X_HEAD_DIM, D_MODEL), (X_HEADS * X_HEAD_DIM) ** -0.5),
        "ffn_norm_g": gain(ks[15], (DEPTH_2, D_MODEL)),
        "w_ffn_gate": nrm(ks[16], (DEPTH_2, D_MODEL, D_FF), D_MODEL ** -0.5),
        "w_ffn_up": nrm(ks[17], (DEPTH_2, D_MODEL, D_FF), D_MODEL ** -0.5),
        "w_ffn_down": nrm(ks[18], (DEPTH_2, D_FF, D_MODEL), D_FF ** -0.5),
        "final_norm_g": gain(ks[19], (D_MODEL,)),
    }

def second_block(x, mem, mix_norm_g, w_in, forget_bias, conv_w, sink, w_branch, w_mix_out,
              rel_bias, xattn_norm_g, mem_norm_g, w_xq, w_xkv, w_xo, ffn_norm_g,
              w_ffn_gate, w_ffn_up, w_ffn_down, final_norm_g):
    b, s = x.shape[0], x.shape[1]
    for l in range(DEPTH_2):
        h = rms_norm_2(x, mix_norm_g[l])
        (c_b, c_c, c_u, f_q, f_k, f_v, f_g, s_q, s_k, s_v, gate_logits) = split_proj(h @ w_in[l])
        y_conv = short_conv_branch(c_b, c_c, c_u, conv_w[l])
        y_fox = fox_branch(f_q, f_k, f_v, f_g, forget_bias[l])
        y_swa = swa_sink_branch(s_q, s_k, s_v, rel_bias, sink[l])
        gates = jax.nn.sigmoid(gate_logits.reshape(b, s, N_BRANCH, D_MODEL))
        merged = (gates[:, :, 0] * (y_conv @ w_branch[l, 0])
                  + gates[:, :, 1] * (y_fox @ w_branch[l, 1])
                  + gates[:, :, 2] * (y_swa @ w_branch[l, 2]))
        x = x + merged @ w_mix_out[l]
        x = x + cross_attention(rms_norm_2(x, xattn_norm_g[l]), rms_norm_2(mem, mem_norm_g[l]),
                                w_xq[l], w_xkv[l], w_xo[l])
        x = x + swiglu(rms_norm_2(x, ffn_norm_g[l]), w_ffn_gate[l], w_ffn_up[l], w_ffn_down[l])
    return rms_norm_2(x, final_norm_g)


def setup_inputs(seed=0):
    out = dict(first_inputs(seed))
    for name, value in second_inputs(seed + 1).items():
        if name != "x":
            out[name + "_2"] = value
    return out


def reference(
    x, ssm_ln_g, ssm_in_w, ssm_conv_w, ssm_conv_b, ssm_dt_bias, ssm_a_log, ssm_d, ssm_norm_g,
    ssm_out_w, kv_ln_g, kv_w, k_norm_g, rel_bias, attn_ln_g, q_w, q_norm_g, lam_vecs, subln_g,
    attn_out_w, ffn_ln_g, ffn_up_w, ffn_conv_w, ffn_conv_b, ffn_down_w, mem_2, mix_norm_g_2,
    w_in_2, forget_bias_2, conv_w_2, sink_2, w_branch_2, w_mix_out_2, rel_bias_2,
    xattn_norm_g_2, mem_norm_g_2, w_xq_2, w_xkv_2, w_xo_2, ffn_norm_g_2, w_ffn_gate_2,
    w_ffn_up_2, w_ffn_down_2, final_norm_g_2,
):
    x = first_block(
        x, ssm_ln_g, ssm_in_w, ssm_conv_w, ssm_conv_b, ssm_dt_bias, ssm_a_log, ssm_d,
        ssm_norm_g, ssm_out_w, kv_ln_g, kv_w, k_norm_g, rel_bias, attn_ln_g, q_w, q_norm_g,
        lam_vecs, subln_g, attn_out_w, ffn_ln_g, ffn_up_w, ffn_conv_w, ffn_conv_b, ffn_down_w,
    )
    return second_block(
        x, mem_2, mix_norm_g_2, w_in_2, forget_bias_2, conv_w_2, sink_2, w_branch_2,
        w_mix_out_2, rel_bias_2, xattn_norm_g_2, mem_norm_g_2, w_xq_2, w_xkv_2, w_xo_2,
        ffn_norm_g_2, w_ffn_gate_2, w_ffn_up_2, w_ffn_down_2, final_norm_g_2,
    )


_drawn_inputs = setup_inputs


def setup_inputs(seed=0):
    import zlib

    import numpy as np

    out = dict(_drawn_inputs(seed))
    spreads = {}
    factors = {'ssm_d': 4.147,
     'kv_ln_g': 4.07,
     'k_norm_g': 6.009,
     'attn_ln_g': 6.054,
     'q_norm_g': 6.079,
     'subln_g': 6.155,
     'ffn_ln_g': 2.852,
     'ffn_conv_b': 2.835,
     'forget_bias_2': 33.384,
     'sink_2': 23.791,
     'rel_bias_2': 2.76,
     'xattn_norm_g_2': 8.0,
     'mem_norm_g_2': 5.93,
     'ffn_norm_g_2': 7.148}
    for name, (base, spread) in spreads.items():
        noise = np.random.default_rng([zlib.crc32(name.encode()), seed]).standard_normal(out[name].shape)
        drawn = base * np.exp(spread * noise) if base else spread * noise
        out[name] = jnp.asarray(drawn.astype(out[name].dtype))
    for name, factor in factors.items():
        out[name] = (out[name] * factor).astype(out[name].dtype)
    return out
```

```python
from contextlib import ExitStack

import numpy as np

import concourse.bass as bass
from concourse import mybir

F = mybir.dt.float32
R = mybir.dt.float32r
BF = mybir.dt.bfloat16
ALU = mybir.AluOpType
ACT = mybir.ActivationFunctionType
MUL, ADD, SUB, MIN, MAX, POW = ALU.mult, ALU.add, ALU.subtract, ALU.min, ALU.max, ALU.pow

P = 128
S = 512
D = 1024
DC = D // P
NT = S // P
EPS = 1e-6
LAM_INIT = 0.8 - 0.6 * float(np.exp(-0.3))
FFC = 22
BIG = 1e30
FMAX = 3.0e38
ENGINES = ("pe", "act", "dve", "pool", "sp")

N_RAW, N_W, AHEAD = 3, 3, 2
UNIT = 1024


class Tok:

    def __init__(self, eng):
        self.eng, self.used, self.sem, self.val = eng, False, None, 0


class Slot:

    def __init__(self, sem):
        self.sem, self.n = sem, 0


def flat(x):
    if x is None:
        return []
    if isinstance(x, Tok):
        return [x]
    return [t for y in x for t in flat(y)]


class Queues:
    def __init__(self):
        self.q = {e: [] for e in ENGINES}
        self.last = {}

    def op(self, eng, fn, *waits):
        w = flat(waits)
        for t in w:
            t.used = True
        tok = Tok(eng)
        self.q[eng].append((fn, w, tok))
        self.last[eng] = tok
        return tok

    def dma(self, eng, fn, slot, *waits):
        w = flat(waits)
        for t in w:
            t.used = True
        tok = Tok("dma")
        slot.n += 1
        tok.sem, tok.val = slot.sem, 16 * slot.n
        self.q[eng].append((fn, w, tok))
        return tok

    def ends(self):
        return [self.last[e] for e in ("pe", "act", "dve", "pool") if e in self.last]

    def number(self, sems):
        for e in ENGINES:
            n = 0
            for _, _, tok in self.q[e]:
                if tok.eng != "dma" and tok.used:
                    n += 1
                    tok.sem, tok.val = sems[e], n

    def play(self, name, eng):
        seen = {}
        for fn, waits, tok in self.q[name]:
            need = {}
            for t in waits:
                k = id(t.sem)
                if t.val > need.get(k, (None, 0))[1]:
                    need[k] = (t.sem, t.val)
            for k, (sem, val) in need.items():
                if seen.get(k, 0) < val:
                    eng.wait_ge(sem, val)
                    seen[k] = val
            ins = fn(eng)
            if tok.eng == "dma":
                ins.then_inc(tok.sem, 16)
            elif tok.used:
                ins.then_inc(tok.sem, 1)


class Pool:

    def __init__(self, bufs, *after):
        self.free = [(b, flat(after)) for b in bufs]

    def take(self):
        return self.free.pop(0)

    def give(self, buf, *toks):
        self.free.append((buf, flat(toks)))


def t5_bucket(n):
    n = np.maximum(n, 0)
    big = np.maximum(n, 1).astype(np.float32)
    large = 16 + (np.log(big / np.float32(16)) / np.float32(np.log(8.0)) * np.float32(16)).astype(np.int32)
    return np.where(n < 16, n, np.minimum(large, 31))


L1, L2 = 640, 384


def constants():
    i = np.arange(P)
    ident = np.eye(P, dtype=np.float32)
    tri = (i[:, None] <= i[None, :]).astype(np.float32)
    above = np.where(i[None, :] > i[:, None], BIG, 0).astype(np.float32)
    below = np.where(i[None, :] < i[:, None], -BIG, 0).astype(np.float32)
    blk = np.zeros((P, 2), np.float32)
    blk[:64, 0] = blk[64:, 1] = 1
    d1, d2 = 511 - np.arange(L1), 255 - np.arange(L2)
    oh1, oh2 = np.zeros((P, L1), np.float32), np.zeros((P, L2), np.float32)
    ok1, ok2 = d1 >= 0, (d2 >= 0) & (d2 < 128)
    oh1[t5_bucket(d1)[ok1], np.arange(L1)[ok1]] = 1
    oh2[t5_bucket(d2)[ok2], np.arange(L2)[ok2]] = 1
    m1 = np.tile(np.where(ok1, 0, BIG).astype(np.float32), (P, 1))
    m2 = np.tile(np.where(ok2, 0, BIG).astype(np.float32), (P, 1))
    keep = np.concatenate([ident, tri, np.ones((P, P), np.float32), blk], 1)
    once = np.concatenate([above, below, oh1, m1, oh2, m2], 1)
    return keep, once


N_KEEP = 3 * P + 2
N_ONCE = 2 * P + 2 * L1 + 2 * L2

PAR = {}


def _lay():
    at = 0
    for name, n in [
        ("ssm_ln", 8), ("kv_ln", 8), ("attn_ln", 8), ("ffn_ln0", 8), ("ffn_ln1", 8), ("mix", 8), ("xattn", 8),
        ("mem", 8), ("ffn2", 8), ("final", 8), ("scw", 96), ("scb", 24), ("sng", 16), ("sd", 16), ("dtb", 32),
        ("alog", 32), ("kn", 1), ("qn", 1), ("lam", 256), ("subln", 1), ("rel", 8), ("rel2", 8), ("fcw0", 132),
        ("fcb0", 44), ("fcw1", 132), ("fcb1", 44), ("fbias", 8), ("cw2", 12), ("sink", 8),
    ]:
        PAR[name] = (at, n)
        at += n
    return at


N_PAR = _lay()


def cols(v):
    return np.asarray(v).reshape(-1, P).T


def parameters(a):
    def rows(v):
        return np.broadcast_to(np.asarray(v).reshape(1, -1), (P, np.asarray(v).size))

    def taps(w):
        w = np.asarray(w)
        return w.reshape(w.shape[0], -1, P).transpose(2, 1, 0).reshape(P, -1)

    def table(v):
        out = np.zeros((P, 8), np.float32)
        out[:32] = v
        return out

    got = {
        "ssm_ln": cols(a["ssm_ln_g"]), "kv_ln": cols(a["kv_ln_g"]), "attn_ln": cols(a["attn_ln_g"]),
        "ffn_ln0": cols(a["ffn_ln_g"][0]), "ffn_ln1": cols(a["ffn_ln_g"][1]), "mix": cols(a["mix_norm_g_2"]),
        "xattn": cols(a["xattn_norm_g_2"]), "mem": cols(a["mem_norm_g_2"]), "ffn2": cols(a["ffn_norm_g_2"]),
        "final": cols(a["final_norm_g_2"]), "scw": taps(a["ssm_conv_w"][0]), "scb": cols(a["ssm_conv_b"]),
        "sng": cols(a["ssm_norm_g"]), "sd": cols(np.repeat(np.asarray(a["ssm_d"])[0], 64)),
        "dtb": rows(a["ssm_dt_bias"]), "alog": rows(a["ssm_a_log"]),
        "kn": cols(np.tile(a["k_norm_g"], 2)), "qn": cols(np.tile(np.asarray(a["q_norm_g"])[0], 2)),
        "lam": rows(a["lam_vecs"]), "subln": cols(a["subln_g"]), "rel": table(a["rel_bias"]),
        "rel2": table(a["rel_bias_2"]), "fcw0": taps(a["ffn_conv_w"][0]), "fcb0": cols(a["ffn_conv_b"][0]),
        "fcw1": taps(a["ffn_conv_w"][1]), "fcb1": cols(a["ffn_conv_b"][1]), "fbias": rows(a["forget_bias_2"]),
        "cw2": taps(a["conv_w_2"][0]), "sink": rows(a["sink_2"]),
    }
    return np.concatenate([got[k] for k in PAR], 1).astype(np.float32)


class Stop(Exception):
    pass


def emit(nc, ctx, plan, dram, stop=None):
    Q = Queues()
    op = Q.op
    names = [0]

    def sb(scope, shape, dt=F):
        names[0] += 1
        return scope.enter_context(nc.sbuf_tensor(f"t{names[0]}", shape, dt))

    def sem(name):
        return ctx.enter_context(nc.semaphore(name))

    sems = {e: sem(f"done_{e}") for e in ENGINES}

    x = sb(ctx, [P, DC, S])
    XAh, XAl = sb(ctx, [P, DC, S], R), sb(ctx, [P, DC, S], R)
    XBh, XBl = sb(ctx, [P, DC, S], R), sb(ctx, [P, DC, S], R)
    keep = sb(ctx, [P, N_KEEP])
    par = sb(ctx, [P, N_PAR])
    maskb = sb(ctx, [P, 2, P], BF)
    identb = sb(ctx, [P, P], BF)
    mhalf = sb(ctx, [P, 8])
    rsrow = sb(ctx, [P, S])
    acc = sb(ctx, [P, S])
    sqs = [sb(ctx, [P, S]) for _ in range(2)]
    stat = sb(ctx, [P, 4, 8])
    rstok = sb(ctx, [P, 8])
    raws = [sb(ctx, [P, UNIT]) for _ in range(N_RAW)]
    his = [sb(ctx, [P, UNIT], R) for _ in range(N_W)]
    los = [sb(ctx, [P, UNIT], R) for _ in range(N_W)]
    banks = [ctx.enter_context(nc.psum_tensor(f"bank{i}", [P, S], F)) for i in range(8)]
    ident, tri, ones = keep[:, 0:P], keep[:, P:2 * P], keep[:, 2 * P:3 * P]
    blk = keep[:, 3 * P:3 * P + 2]

    def pc(name, i=0, n=1):
        return par[:, PAR[name][0] + i:PAR[name][0] + i + n]

    main, misc = Pool(banks[0:3]), Pool(banks[3:8])
    sq_pool = Pool(sqs)

    def copy_act(out, in_, *w, scale=1.0):
        return op("act", lambda e: e.activation(out, in_, ACT.Copy, scale=scale), *w)

    def func(f, out, in_, *w, bias=0.0, scale=1.0, accum=None):
        return op("act", lambda e: e.activation(out, in_, f, bias=bias, scale=scale, accum_out=accum), *w)

    def tt(out, a, b, o, *w, eng="dve"):
        return op(eng, lambda e: e.tensor_tensor(out, a, b, o), *w)

    def stt(out, a, s, b, o0, o1, *w):
        return op("dve", lambda e: e.scalar_tensor_tensor(out=out, in0=a, scalar=s, in1=b, op0=o0, op1=o1), *w)

    def ts(out, a, s0, s1, o0, o1, *w, eng="dve"):
        if o1 is None:
            return op(eng, lambda e: e.tensor_scalar(out, a, s0, None, o0), *w)
        return op(eng, lambda e: e.tensor_scalar(out, a, s0, s1, o0, o1), *w)

    def recip(out, a, *w):
        return op("dve", lambda e: e.reciprocal(out, a), *w)

    def copy_dve(out, in_, *w):
        return op("dve", lambda e: e.tensor_copy(out, in_), *w)

    def add_min(out, a, b, m, *w):
        return op("dve", lambda e: e.tensor_tensor_reduce(out, a, b, 1.0, FMAX, ADD, MIN, m), *w)

    def mm(out, lhs, rhs, *w, start=True, stop=True, loose=False):
        return op("pe", lambda e: e.matmul(out, lhs, rhs, start=start, stop=stop, skip_group_check=loose), *w)

    def turn(out, in_, *w):
        n = in_.shape[0]
        return op("pe", lambda e: e.transpose(out, in_, ident[0:n, 0:n]), *w)

    def memset(out, v, *w):
        return op("pool", lambda e: e.memset(out, v), *w)

    class Weights:
        def __init__(self):
            self.want, self.u = [], 0
            self.loaded = self.split_ = 0
            self.slots = [Slot(sem(f"w{i}")) for i in range(N_RAW)]
            self.arrived, self.cut, self.done_ = {}, {}, {}

        def load(self, v):
            if v >= len(plan):
                return
            off, n = plan[v][-2:]
            dst = raws[v % N_RAW][:, 0:n]

            def go(e):
                src = dram["w"][off:off + P * n].rearrange("(p n) -> p n", p=P)
                return e.dma_start(dst, src)

            self.arrived[v] = Q.dma("sp", go, self.slots[v % N_RAW], self.cut.get(v - N_RAW))

        def split(self, v):
            n = plan[v][-1]
            raw, hi, lo = raws[v % N_RAW][:, 0:n], his[v % N_W][:, 0:n], los[v % N_W][:, 0:n]
            t = copy_act(hi, raw, self.arrived[v], self.done_.get(v - N_W))
            self.cut[v] = tt(lo, raw, hi.bitcast(F), SUB, t, self.done_.get(v - N_W))

        def unit(self, name, r0, nk, c0, nc_):
            n = nk * nc_
            self.want.append((name, r0, nk, c0, nc_))
            u, self.u = self.u, self.u + 1
            if plan is not None:
                assert plan[u][:5] == (name, r0, nk, c0, nc_)
                while self.loaded < N_RAW:
                    self.load(self.loaded)
                    self.loaded += 1
                while self.split_ <= min(u + AHEAD, len(plan) - 1):
                    self.split(self.split_)
                    self.load(self.loaded)
                    self.loaded += 1
                    self.split_ += 1
            v = (t[u % N_W][:, 0:n].rearrange("p (k n) -> p k n", k=nk) for t in (his, los))
            return u, *v, self.cut.get(u)

        def done(self, u, tok):
            self.done_[u] = tok

    W = Weights()

    def proj(out, name, c0, X, nk, *w, per=8, ncol=P, start=True, stop=True):
        tok = None
        for r0 in range(0, nk, per):
            k = min(per, nk - r0)
            u, wh, wl, tw = W.unit(name, r0, k, c0, ncol)
            for c in range(k):
                xh, xl, tx = X[r0 + c]
                first, last = start and r0 + c == 0, stop and r0 + c == nk - 1
                mm(out, wl[:, c, :], xh, tw, tx, w, start=first, stop=False)
                mm(out, wh[:, c, :], xl, start=False, stop=False)
                tok = mm(out, wh[:, c, :], xh, start=False, stop=last)
            W.done(u, tok)
        return tok

    def proj_tok(outs, name, c0, ncol, X, nk, per, *w):
        toks = [None] * len(outs)
        for r0 in range(0, nk, per):
            u, wh, wl, tw = W.unit(name, r0, per, c0, ncol)
            for j, out in enumerate(outs):
                for c in range(per):
                    xh, xl, tx = X[r0 + c]
                    a = slice(j * P, j * P + P)
                    mm(out, xh[:, a], wl[:, c, :], tw, tx, w, start=r0 + c == 0, stop=False)
                    mm(out, xl[:, a], wh[:, c, :], start=False, stop=False)
                    toks[j] = mm(out, xh[:, a], wh[:, c, :], start=False, stop=r0 + c == nk - 1)
            W.done(u, toks[-1])
        return toks

    rs_state = {"row": [], "stat": [], "acc": []}

    def inv_rms(a, t_a, scale, row, row_free, groups=1, width=S, tok_out=None):
        nt = width // P
        bank, free = misc.take()
        rhs = ones[:, 0:1] if groups == 1 else blk
        g = groups
        for j in range(nt):
            t = mm(bank[:, j * g:j * g + g], a[:, j * P:j * P + P], rhs, t_a, free)
        ms, dst = stat[:, 0, 0:nt * g], (rstok[:, 0:nt * g] if tok_out is None else tok_out)
        t = ts(ms, bank[:, 0:nt * g], scale, EPS, MUL, ADD, t, rs_state["stat"])
        t_p = op("pool", lambda e: e.tensor_tensor(dst, ms, mhalf[:, 0:nt * g], POW), t, t_mhalf, rs_state["stat"])
        for j in range(nt):
            for i in range(g):
                r = slice(64 * i, 64 * i + P // g)
                t = mm(bank[r, j * P:j * P + P], dst[:, g * j + i:g * j + i + 1].to_broadcast([P, P // g]), ident, t_p)
        rs_state["stat"] = [t, t_p]
        t_row = copy_act(row[:, 0:width], bank[:, 0:width], t, row_free)
        misc.give(bank, t_row)
        return t_row, t_p

    class Norm:

        def __init__(self, gain, Xh, Xl, free):
            self.gain, self.Xh, self.Xl, self.free = gain, Xh, Xl, free
            self.X, self.t = [], None

        def chunk(self, c, t_x):
            g, h, lo = pc(self.gain, c), self.Xh[:, c, :], self.Xl[:, c, :]
            sq, fr = sq_pool.take()
            t_h = copy_act(h, x[:, c, :], t_x, self.free, scale=g)
            t_l = stt(lo, x[:, c, :], g, h.bitcast(F), MUL, SUB, t_h, self.free)
            if c == 0:
                t_s = self.t = func(ACT.Square, acc[:, :], x[:, c, :], t_x, rs_state["acc"])
                sq_pool.give(sq, fr)
            else:
                t_s = func(ACT.Square, sq[:, :], x[:, c, :], t_x, fr)
                self.t = tt(acc[:, :], acc[:, :], sq[:, :], ADD, t_s, self.t, eng="pool")
                sq_pool.give(sq, self.t)
            self.X.append((h, lo, t_l))
            return [t_l, t_s]

        def finish(self):
            t_row, t_tok = inv_rms(acc, self.t, 1.0 / D, rsrow, rs_state["row"])
            rs_state["acc"] = [t_row]
            rs_state["row"] = []
            return t_row, t_tok

    def leave_rows(*toks):
        rs_state["row"] = rs_state["row"] + flat(toks)

    def add_to_x(c, bank, t, t_x):
        t1 = tt(x[:, c, :], bank[:, :], x[:, c, :], ADD, t, t_x)
        main.give(bank, t1)
        return t1

    def store_x(toks, slot):
        return Q.dma("sp", lambda e: e.dma_start(dram["out"].rearrange("(c p) n -> p c n", p=P), x[:, :, :]),
                     slot, toks)

    s_out = Slot(sem("s_out"))
    s_in = [Slot(sem(f"s_in{i}")) for i in range(4)]

    t_keep = Q.dma("act", lambda e: e.dma_start(keep[:, :], dram["keep"]), s_in[0])
    t_par = Q.dma("act", lambda e: e.dma_start(par[:, :], dram["par"]), s_in[1])
    t_xin = [Q.dma("sp", lambda e, c=c: e.dma_start(x[:, c, :], dram["x"][c * P:c * P + P, :]),
                   Slot(sem(f"s_x{c}"))) for c in range(DC)]
    t_mhalf = memset(mhalf[:, :], -0.5)
    zero_par = [t_keep, t_par]

    def fence(*toks):
        return flat(toks)

    setup = ExitStack()
    once = sb(setup, [P, N_ONCE])
    tabs = [sb(setup, [P, L1]) for _ in range(2)]
    t_once = Q.dma("act", lambda e: e.dma_start(once[:, :], dram["once"]), s_in[2])
    t_id = copy_dve(identb[:, :], ident, t_keep)
    t_mk = copy_dve(maskb[:, :, :], once[:, 0:2 * P].rearrange("p (a b) -> p a b", a=2), t_once)
    o = 2 * P
    oh1, m1, oh2, m2 = (once[:, o:o + L1], once[:, o + L1:o + 2 * L1], once[:, o + 2 * L1:o + 2 * L1 + L2],
                        once[:, o + 2 * L1 + L2:o + 2 * L1 + 2 * L2])
    tab_pool = Pool(tabs)
    s_tab = [Slot(sem("s_tab0")), Slot(sem("s_tab1"))]
    t_tabs = []
    for h in range(16):
        oh, m, ln, rel = (oh1, m1, L1, "rel") if h < 8 else (oh2, m2, L2, "rel2")
        tab, fr = tab_pool.take()
        lhs = pc(rel, h % 8)[0:32, :].to_broadcast([32, P])
        for a in range(0, ln, 320):
            n = min(320, ln - a)
            bank, bf = misc.take()
            t = mm(bank[:, 0:n], lhs, oh[0:32, a:a + n], bf, t_once, t_par)
            t = tt(tab[:, a:a + n], m[:, a:a + n], bank[:, 0:n], SUB, t, fr)
            misc.give(bank, t)

        def put(e, h=h, ln=ln, tab=tab):
            return e.dma_start(dram["tab1" if h < 8 else "tab2"][h % 8], tab[:, 0:ln])

        t_d = Q.dma("act", put, s_tab[h % 2], t)
        t_tabs.append(t_d)
        tab_pool.give(tab, t_d)
    setup.close()
    before = [Q.ends(), t_tabs[-2:]]
    t_const = [t_keep, t_par, t_id, t_mk]

    A = ExitStack()
    XS = [sb(A, [P, 4, S]) for _ in range(2)]
    BC = [sb(A, [P, 2, S]) for _ in range(2)]
    Btok, cbm = sb(A, [P, NT, P]), sb(A, [P, NT, P])
    xdt, xds = sb(A, [P, NT, S]), sb(A, [P, 3, S])
    St = sb(A, [P, 3, S])
    ZT = sb(A, [P, 4, S])
    hd = Pool([sb(A, [P, S]) for _ in range(4)], before)
    ep = Pool([sb(A, [P, S]) for _ in range(1)], before)
    us = [sb(A, [P, S + 4]) for _ in range(2)]
    rg = sb(A, [P, S])
    csT = sb(A, [32, S])
    dts, asb, css, dst_, ctot = (sb(A, [P, NT * 32]) for _ in range(5))
    rg_tok = sb(A, [P, 8])

    t_pad = [memset(u[:, 0:4], 0.0, before) for u in us]
    u_pool = Pool(us, t_pad, before)

    n1 = Norm("ssm_ln", XAh, XAl, None)
    n1_toks = []
    for c in range(DC):
        n1_toks += n1.chunk(c, [t_xin[c], t_const])
    t_row, t_tok = n1.finish()
    X = n1.X

    bank, bf = main.take()
    u, wh, wl, tw = W.unit("ssm_in", 0, 8, 5120, 32)
    for j in range(NT):
        for c in range(DC):
            a = slice(j * P, j * P + P)
            o_ = bank[:, 32 * j:32 * j + 32]
            mm(o_, X[c][0][:, a], wl[:, c, :], tw, X[c][2], bf, start=c == 0, stop=False)
            mm(o_, X[c][1][:, a], wh[:, c, :], start=False, stop=False)
            t = mm(o_, X[c][0][:, a], wh[:, c, :], start=False, stop=c == DC - 1)
    W.done(u, t)
    for j in range(NT):
        b = slice(32 * j, 32 * j + 32)
        t = stt(dts[:, b], bank[:, b], rstok[:, j:j + 1], pc("dtb", 0, 32), MUL, ADD, t, t_tok, before)
    main.give(bank, t)
    leave_rows(t)
    t_v = t
    t = ts(asb[:, :], dts[:, :], -1.0, None, MUL, None, t_v, before)
    t = tt(asb[:, :], asb[:, :], dts[:, :], MIN, t)
    t = func(ACT.Exp, asb[:, :], asb[:, :], t)
    t_ea = func(ACT.Exp, ctot[:, 0:32], pc("alog", 0, 32), before)
    t = func(ACT.Ln, asb[:, :], asb[:, :], t, bias=1.0)
    t_dt = stt(dts[:, :], dts[:, :], 0.0, asb[:, :], MAX, ADD, t)
    for j in range(NT):
        b = slice(32 * j, 32 * j + 32)
        t = stt(asb[:, b], dts[:, b], -1.0, ctot[:, 0:32], MUL, MUL, t_dt, t_ea)
    t_a = t
    bank, bf = misc.take()
    mm(bank[:, 0:P], tri, asb[:, :], bf, t_a)
    t = mm(bank[:, P:2 * P], ones, asb[:, :])
    t_cs = copy_act(css[:, :], bank[:, 0:P], t, before)
    t_sub = tt(dst_[:, :], bank[:, P:2 * P], css[:, :], SUB, t_cs, before)
    t_ct = func(ACT.Exp, ctot[:, :], bank[:, P:2 * P], t_sub, t_a)
    misc.give(bank, t_ct)
    t_ds = func(ACT.Exp, dst_[:, :], dst_[:, :], t_sub)
    bank, bf = misc.take()
    for j in range(NT):
        t = turn(bank[0:32, j * P:j * P + P], css[:, 32 * j:32 * j + 32], bf, t_cs)
    t_csT = copy_act(csT[:, :], bank[0:32, :], t, before)
    misc.give(bank, t_csT)

    y_free = [None] * 4
    xs_free = [[before, None], [before, None]]
    st = {"xs": [flat(before), flat(before)], "bc": [flat(before), flat(before)], "btok": flat(before),
          "cbm": flat(before), "xdt": flat(before), "xds": flat(before), "St": flat(before), "zt": flat(before),
          "rg": flat(before), "y": [[], []]}

    def conv_silu(ft, dst, dst_free):
        bank, bf = main.take()
        t = proj(bank[:, :], "ssm_in", 2048 + ft * P, X, DC, bf)
        ub, uf = u_pool.take()
        t1 = tt(ub[:, 4:S + 4], bank[:, :], rsrow[:, :], MUL, t, t_row, uf)
        main.give(bank, t1)
        leave_rows(t1)
        t = func(ACT.Identity, dst, ub[:, 1:S + 1], t1, dst_free, bias=pc("scb", ft), scale=pc("scw", 4 * ft))
        for k in range(1, 4):
            t = stt(dst, ub[:, 1 + k:S + 1 + k], pc("scw", 4 * ft + k), dst, MUL, ADD, t)
        u_pool.give(ub, t)
        return func(ACT.Silu, dst, dst, t)

    def group_in(g):
        b = g % 2
        st["in", g] = {}

        def one(i):
            if i < 2:
                t = conv_silu(16 + 4 * i + g, BC[b][:, i, :], st["bc"][b])
            else:
                t = conv_silu(4 * g + i - 2, XS[b][:, i - 2, :], st["xs"][b])
            st["in", g][i] = t

        return [lambda i=i: one(i) for i in range(6)]

    def group_z(g):
        st["z", g] = {}

        def one(i):
            bank, bf = main.take()
            t = proj(bank[:, :], "ssm_in", (4 * g + i) * P, X, DC, bf)
            t1 = tt(ZT[:, i, :], bank[:, :], rsrow[:, :], MUL, t, t_row, st["zt"])
            main.give(bank, t1)
            leave_rows(t1)
            st["z", g][i] = func(ACT.Silu, ZT[:, i, :], ZT[:, i, :], t1)

        return [lambda i=i: one(i) for i in range(4)]

    def ssd(g):
        b = g % 2
        got = st["in", g]
        BT, CT = BC[b][:, 0, :], BC[b][:, 1, :]
        bank, bf = misc.take()
        for c in range(NT):
            t = turn(bank[:, c * P:c * P + P], BT[:, c * P:c * P + P], bf, got[0])
        t_bt = copy_act(Btok[:, :, :], bank[:, :].rearrange("p (c n) -> p c n", c=NT), t, st["btok"])
        misc.give(bank, t_bt)
        yield
        bank, bf = misc.take()
        for c in range(NT):
            a = slice(c * P, c * P + P)
            t = mm(bank[:, a], BT[:, a], CT[:, a], bf, got[0], got[1])
        t_cb = tt(cbm[:, :, :], bank[:, :].rearrange("p (c n) -> p c n", c=NT),
                  tri.unsqueeze(1).to_broadcast([P, NT, P]), MUL, t, st["cbm"])
        misc.give(bank, t_cb)
        yield
        t_xdt, t_xds = [], []
        for c in range(NT):
            bank, bf = misc.take()
            for i in range(4):
                t = turn(bank[:, i * P:i * P + P], XS[b][:, i, c * P:c * P + P], bf, got[2 + i])
            hs = slice(32 * c + 8 * g, 32 * c + 8 * g + 8)
            t = tt(xdt[:, c, :].rearrange("p (h d) -> p h d", h=8), bank[:, :].rearrange("p (h d) -> p h d", h=8),
                   dts[:, hs].unsqueeze(2).to_broadcast([P, 8, 64]), MUL, t, t_dt, st["xdt"])
            misc.give(bank, t)
            t_xdt.append(t)
            if c < 3:
                t = tt(xds[:, c, :].rearrange("p (h d) -> p h d", h=8), xdt[:, c, :].rearrange("p (h d) -> p h d", h=8),
                       dst_[:, hs].unsqueeze(2).to_broadcast([P, 8, 64]), MUL, t, t_ds, st["xds"], eng="pool")
                t_xds.append(t)
            yield
        t_S = []
        for c in range(3):
            bank, bf = misc.take()
            t = mm(bank[:, :], Btok[:, c, :], xds[:, c, :], bf, t_bt, t_xds[c])
            if c == 0:
                t = copy_act(St[:, 0, :], bank[:, :], t, st["St"])
            else:
                hs = slice(32 * c + 8 * g, 32 * c + 8 * g + 8)
                t_m = tt(St[:, c, :].rearrange("p (h d) -> p h d", h=8),
                         St[:, c - 1, :].rearrange("p (h d) -> p h d", h=8),
                         ctot[:, hs].unsqueeze(2).to_broadcast([P, 8, 64]), MUL, t_S[-1], t_ct, st["St"], eng="pool")
                t = tt(St[:, c, :], bank[:, :], St[:, c, :], ADD, t, t_m)
            misc.give(bank, t)
            t_S.append(t)
            yield
        st["btok"] = st["xds"] = [t_S[-1]]
        t_y, t_g = [], []
        for pair in range(4):
            Ds = []
            for k in range(2):
                h = 8 * g + 2 * pair + k
                bank, bf = misc.take()
                mm(bank[:, :], ident[0:32, h:h + 1].to_broadcast([32, P]), csT[:, :], bf, t_csT, stop=False)
                for c in range(NT):
                    t = mm(bank[:, c * P:c * P + P], identb[:, :], maskb[:, 1, :], t_id, t_mk, start=False,
                           stop=c == NT - 1)
                d, df = hd.take()
                d3 = d[:, :].rearrange("p (c n) -> p c n", c=NT)
                cs_h = css[:, h:h + 97:32].unsqueeze(2).to_broadcast([P, NT, P])
                t = tt(d3, bank[:, :].rearrange("p (c n) -> p c n", c=NT), cs_h, SUB, t, t_cs, df)
                misc.give(bank, t)
                Ds.append((d, t))
            bank, bf = misc.take()
            h = 8 * g + 2 * pair
            for k in range(2):
                t_e = mm(bank[64 * k:64 * k + 64, :], ident[0:32, h + k:h + k + 1].to_broadcast([32, 64]), csT[:, :], bf, t_csT)
            yield
            Gs = []
            for d, t in Ds:
                t = func(ACT.Exp, d[:, :], d[:, :], t)
                t = tt(d[:, :], d[:, :], cbm[:, :, :].rearrange("p c n -> p (c n)"), MUL, t, t_cb, eng="pool")
                Gs.append((d, t))
            e_, ef = ep.take()
            t_e = func(ACT.Exp, e_[:, :], bank[:, :], t_e, ef)
            misc.give(bank, t_e)
            yield
            bo, bof = misc.take()
            for c in range(1, NT):
                t_o = mm(bo[:, c * P:c * P + P], St[:, c - 1, pair * P:pair * P + P], CT[:, c * P:c * P + P], bof,
                         t_S[c - 1], got[1])
            by, byf = misc.take()
            for k in range(2):
                d, t = Gs[k]
                for c in range(NT):
                    hl = 2 * pair + k
                    t_m = mm(by[64 * k:64 * k + 64, c * P:c * P + P], xdt[:, c, 64 * hl:64 * hl + 64],
                             d[:, c * P:c * P + P], byf, t, t_xdt[c])
                hd.give(d, t_m)
            xs = XS[b][:, pair, :]
            t_1 = stt(xs, xs, pc("sd", 4 * g + pair), by[:, :], MUL, ADD, t_m, t_xdt, got[2 + pair])
            misc.give(by, t_1)
            t_2 = tt(e_[:, P:S], bo[:, P:S], e_[:, P:S], MUL, t_o, t_e)
            misc.give(bo, t_2)
            t_3 = tt(xs[:, P:S], xs[:, P:S], e_[:, P:S], ADD, t_1, t_2, eng="pool")
            ep.give(e_, t_3)
            t_y.append([t_1, t_3])
            t_g.append([t_m, t_o])
            yield
        st["cbm"] = [t for _, t in Gs] + flat(t_g[-1])
        st["xdt"] = st["St"] = flat(t_g)
        st["bc"][b] = flat(t_g)
        st["ty", g] = t_y

    def group_out(g):
        b = g % 2
        t_a = None
        ty = []
        for i in range(4):
            xs = XS[b][:, i, :]
            t = tt(xs, xs, ZT[:, i, :], MUL, st["ty", g][i], st["z", g][i], eng="pool")
            sq, fr = sq_pool.take()
            if i == 0:
                t_a = func(ACT.Square, acc[:, :], xs, t, rs_state["acc"])
                sq_pool.give(sq, fr)
            else:
                t_s = func(ACT.Square, sq[:, :], xs, t, fr)
                t_a = tt(acc[:, :], acc[:, :], sq[:, :], ADD, t_s, t_a, eng="pool")
                sq_pool.give(sq, t_a)
            ty.append(t)
        st["zt"] = flat(ty)
        yield
        t_r, _ = inv_rms(acc, t_a, 1.0 / 512, rg, st["rg"], tok_out=rg_tok[:, 0:4])
        rs_state["acc"] = [t_r]
        yield
        Y = []
        for i in range(4):
            xs = XS[b][:, i, :]
            h, lo = XBh[:, 4 * b + i, :], XBl[:, 4 * b + i, :]
            t = stt(xs, xs, pc("sng", 4 * g + i), rg[:, :], MUL, MUL, t_r, ty[i])
            st["rg"] = [t]
            t_h = copy_act(h, xs, t, st["y"][b])
            t_l = tt(lo, xs, h.bitcast(F), SUB, t_h, st["y"][b])
            Y.append((h, lo, t_l))
        st["xs"][b] = [t_l]
        st["Y", g] = Y
        yield

    x_tok = [n1_toks] * DC

    def out_jobs(g, post=None):
        Y = st["Y", g]

        def one(pairt):
            bk = [main.take(), main.take()]
            u, wh, wl, tw = W.unit("ssm_out", 4 * g, 4, 2 * pairt * P, 2 * P)
            toks = []
            for k in range(2):
                for c in range(4):
                    yh, yl, ty = Y[c]
                    a = slice(k * P, k * P + P)
                    mm(bk[k][0][:, :], wl[:, c, a], yh, tw, ty, bk[k][1], start=c == 0, stop=False)
                    mm(bk[k][0][:, :], wh[:, c, a], yl, start=False, stop=False)
                    t = mm(bk[k][0][:, :], wh[:, c, a], yh, start=False, stop=c == 3)
                toks.append(t)
            W.done(u, t)
            st["y"][g % 2] = [t]
            for k in range(2):
                c = 2 * pairt + k
                x_tok[c] = [add_to_x(c, bk[k][0], toks[k], x_tok[c])]
                if post:
                    post(c, x_tok[c])

        return [lambda i=i: one(i) for i in range(4)]

    def weave(jobs, side, ratio=1):
        side = iter(side)
        for j in jobs:
            j()
            for _ in range(ratio):
                next(side, None)
        for _ in side:
            pass

    def chain(*gens):
        for gen in gens:
            yield from gen

    def lazily(fn, *a):
        yield from fn(*a)

    for j in group_in(0):
        j()
    for g in range(4):
        jobs = group_z(g)
        if g > 0:
            jobs = jobs + out_jobs(g - 1)
        if g < 3:
            jobs = jobs + group_in(g + 1)
        weave(jobs, chain(ssd(g), lazily(group_out, g)), 2)
    nf = Norm("ffn_ln0", XAh, XAl, [st["z", 3][3], Q.last["pe"]])
    for j in out_jobs(3, lambda c, t: x_tok.__setitem__(c, t + nf.chunk(c, t))):
        j()
    A.close()
    rows = nf.finish()

    def check_stop(name):
        if stop == name:
            store_x([x_tok], s_out)
            raise Stop(Q, W, sems, s_out)

    def ffn(up, gate_cols, up_name, up_cols, down, X, t_row, conv, post):
        sc = ExitStack()
        before = Q.ends()
        Hh, Hl = sb(sc, [P, 12, S], R), sb(sc, [P, 12, S], R)
        us = [sb(sc, [P, S + 4]) for _ in range(2)]
        t_pad = [memset(u[:, 0:4], 0.0, before) for u in us]
        u_pool = Pool(us, t_pad, before)
        v_pool = Pool([sb(sc, [P, S]) for _ in range(5)], before)
        h_free = [flat(before) for _ in range(12)]

        def half(name, ft, col):
            bank, bf = main.take()
            t = proj(bank[:, :], name, col + ft % FFC * P, X, DC, bf)
            v, vf = v_pool.take()
            if conv is None:
                t1 = tt(v[:, :], bank[:, :], rsrow[:, :], MUL, t, t_row, vf)
                main.give(bank, t1)
                leave_rows(t1)
                return v, t1
            ub, uf = u_pool.take()
            t1 = tt(ub[:, 4:S + 4], bank[:, :], rsrow[:, :], MUL, t, t_row, uf)
            main.give(bank, t1)
            leave_rows(t1)
            cw, cb = conv
            t = func(ACT.Identity, v[:, :], ub[:, 2:S + 2], t1, vf, bias=pc(cb, ft), scale=pc(cw, 3 * ft))
            for k in (1, 2):
                t = stt(v[:, :], ub[:, 2 + k:S + 2 + k], pc(cw, 3 * ft + k), v[:, :], MUL, ADD, t)
            u_pool.give(ub, t)
            return v, t

        for f0, nf_ in ((0, 12), (12, 10)):
            H = []
            for f in range(f0, f0 + nf_):
                a, t_a = half(up, f, gate_cols)
                t_a = func(ACT.Silu, a[:, :], a[:, :], t_a)
                b, t_b = half(up_name, FFC + f, up_cols)
                t = tt(b[:, :], b[:, :], a[:, :], MUL, t_a, t_b, eng="pool")
                v_pool.give(a, t)
                i = f - f0
                h, lo = Hh[:, i, :], Hl[:, i, :]
                t_h = copy_act(h, b[:, :], t, h_free[i])
                t_l = tt(lo, b[:, :], h.bitcast(F), SUB, t_h, h_free[i])
                v_pool.give(b, t_l)
                H.append((h, lo, t_l))
            for c in range(DC):
                bank, bf = main.take()
                tok = None
                per = nf_ // 2
                for r in range(2):
                    u, wh, wl, tw = W.unit(down, f0 + r * per, per, c * P, P)
                    for k in range(per):
                        xh, xl, tx = H[r * per + k]
                        i0 = r == 0 and k == 0
                        mm(bank[:, :], wl[:, k, :], xh, tw, tx, bf, start=i0, stop=False)
                        mm(bank[:, :], wh[:, k, :], xl, start=False, stop=False)
                        tok = mm(bank[:, :], wh[:, k, :], xh, start=False, stop=r == 1 and k == per - 1)
                    W.done(u, tok)
                x_tok[c] = [add_to_x(c, bank, tok, x_tok[c])]
                if f0 and post:
                    post(c)
            for i in range(12):
                h_free[i] = [tok]
        sc.close()

    def norm_post(n):
        return lambda c: x_tok.__setitem__(c, x_tok[c] + n.chunk(c, x_tok[c]))

    check_stop("mamba")
    X = nf.X
    nq = Norm("attn_ln", XAh, XAl, None)

    class Late:
        pass

    def run_ffn(up, gc, un, uc, down, X, rows, conv, n):
        def post(c):
            if n.free is None:
                n.free = [Q.last["pe"]]
            norm_post(n)(c)
        ffn(up, gc, un, uc, down, X, rows[0], conv, post)

    run_ffn("up0", 0, "up0", 2816, "down0", X, rows, ("fcw0", "fcb0"), nq)
    rows = nq.finish()
    check_stop("ffn0")

    C = ExitStack()
    before = Q.ends()
    t_row, t_tok = rows
    Qf, V = sb(C, [P, 8, S]), sb(C, [P, NT, D])
    kp = Pool([sb(C, [P, S]) for _ in range(2)], before)
    tbp = Pool([sb(C, [P, S]) for _ in range(2)], before)
    s_tb = [Slot(sem(f"s_tb{i}")) for i in range(2)]
    Lp = Pool([sb(C, [P, S]) for _ in range(4)], before)
    ATp = Pool([sb(C, [P, NT, S]) for _ in range(1)], before)
    Op = Pool([sb(C, [P, S]) for _ in range(2)], before)
    sm = Pool([sb(C, [P, 8]) for _ in range(6)], before)
    lamt = sb(C, [P, 64])
    l4 = sb(C, [P, 8])
    rqp = Pool([sb(C, [P, S]) for _ in range(2)], before)
    qscale = sb(C, [P, 1])
    sbl = sb(C, [P, 1])

    t1 = tt(lamt[:, :], pc("lam", 0, 64), pc("lam", 64, 64), MUL, before)
    t1 = op("dve", lambda e: e.tensor_reduce(l4[:, 0:1], lamt[:, :], mybir.AxisListType.X, ADD), t1, before)
    t2 = tt(lamt[:, :], pc("lam", 128, 64), pc("lam", 192, 64), MUL, t1)
    t2 = op("dve", lambda e: e.tensor_reduce(l4[:, 1:2], lamt[:, :], mybir.AxisListType.X, ADD), t2)
    t3 = func(ACT.Exp, l4[:, 2:4], l4[:, 0:2], t2)
    t4 = tt(l4[:, 4:5], l4[:, 2:3], l4[:, 3:4], SUB, t3)
    t_lam = ts(l4[:, 5:6], l4[:, 4:5], LAM_INIT, None, ADD, None, t4)
    t_qs = ts(qscale[:, :], pc("qn"), -0.125, None, MUL, None, before)
    t_sb = ts(sbl[:, :], pc("subln"), 1.0 - LAM_INIT, None, MUL, None, before)

    def head_norm(bank, t, gain, t_gain, dst, dst_free, row_free_extra=None):
        t1 = tt(dst, bank[:, :], rsrow[:, :], MUL, t, t_row, dst_free)
        main.give(bank, t1)
        leave_rows(t1)
        sq, fr = sq_pool.take()
        t_s = func(ACT.Square, sq[:, :], dst, t1, fr)
        rq, rf = rqp.take()
        t8, tf = sm.take()
        t_r, _ = inv_rms(sq, [t_s, tf], 1.0 / 64, rq, rf, groups=2, tok_out=t8[:, 0:8])
        sm.give(t8, t_r)
        sq_pool.give(sq, t_r)
        t2 = stt(dst, dst, gain, rq[:, :], MUL, MUL, t_r, t_gain, t1)
        rqp.give(rq, t2)
        return t2

    nkv = []
    for c in range(DC):
        g, h, lo = pc("kv_ln", c), XBh[:, c, :], XBl[:, c, :]
        t_h = copy_act(h, x[:, c, :], x_tok[c], before, st["y"], scale=g)
        t_l = stt(lo, x[:, c, :], g, h.bitcast(F), MUL, SUB, t_h, before, st["y"])
        x_tok[c] = x_tok[c] + [t_l]
        nkv.append((h, lo, t_l))

    t_q = []
    for h in range(8):
        bank, bf = main.take()
        t = proj(bank[:, :], "q_w", h * P, nq.X, DC, bf)
        t_q.append(head_norm(bank, t, qscale[:, :], t_qs, Qf[:, h, :], before))
    t_qlast = Q.last["pe"]
    t_v = []
    for half in range(2):
        bk = [misc.take() for _ in range(NT)]
        ts_ = proj_tok([b[:, :] for b, _ in bk], "kv_w", D + 512 * half, 512, nkv, DC, 2, [f for _, f in bk])
        for j in range(NT):
            t = copy_act(V[:, j, 512 * half:512 * half + 512], bk[j][0][:, :], ts_[j], t_tok, before,
                         scale=rstok[:, j:j + 1])
            misc.give(bk[j][0], t)
            t_v.append(t)
    leave_rows(t_v)
    rs_state["stat"] = rs_state["stat"] + t_v[-4:]

    def diff_k(h):
        bank, bf = main.take()
        t = proj(bank[:, :], "kv_w", h * P, nkv, DC, bf)
        k, kf = kp.take()
        t = head_norm(bank, t, pc("kn"), None, k[:, :], kf)
        st["k", h] = (k, t)

    def diff_bias(h):
        tb, tbf = tbp.take()

        def get(e):
            flat_ = dram["tab1"][h].rearrange("p n -> (p n)")
            return e.dma_start(tb[:, :], flat_[127:127 + P * (L1 - 1)].rearrange("(p n) -> p n", n=L1 - 1)[:, 0:S])

        st["tb", h] = (tb, Q.dma("act", get, s_tb[h % 2], tbf, t_tabs))

    o_out = []

    def diff_head(h):
        k, t_k = st["k", h]
        tb, t_tb = st["tb", h]
        AT, atf = ATp.take()
        t_at = []
        for i in range(NT):
            n = (i + 1) * P
            Ls, st8 = [], sm.take()
            s8, sf = st8
            tden = []
            for c in range(2):
                bank, bf = misc.take()
                r = slice(64 * c, 64 * c + 64)
                t = mm(bank[:, 0:n], Qf[r, h, i * P:i * P + P], k[r, 0:n], bf, t_q[h], t_k)
                lb, lf = Lp.take()
                t = add_min(lb[:, 0:n], bank[:, 0:n], tb[:, (3 - i) * P:(3 - i) * P + n], s8[:, c:c + 1], t, t_tb, lf, sf)
                misc.give(bank, t)
                t = func(ACT.Exp, lb[:, 0:n], lb[:, 0:n], t, bias=s8[:, c:c + 1], scale=-1.0, accum=s8[:, 2 + c:3 + c])
                Ls.append(lb)
                tden.append(t)
            yield
            t = recip(s8[:, 4:6], s8[:, 2:4], tden)
            t_l = tt(s8[:, 6:7], s8[:, 5:6], l4[:, 5:6], MUL, t, t_lam)
            t_p = ts(Ls[1][:, 0:n], Ls[1][:, 0:n], s8[:, 6:7], 1.0, MUL, MUL, t_l, eng="pool")
            t_a = stt(Ls[0][:, 0:n], Ls[0][:, 0:n], s8[:, 4:5], Ls[1][:, 0:n], MUL, SUB, t_p, t)
            Lp.give(Ls[1], t_a)
            sm.give(s8, t_a)
            bank, bf = misc.take()
            for j in range(i + 1):
                t = turn(bank[:, j * P:j * P + P], Ls[0][:, j * P:j * P + P], t_a, bf)
            Lp.give(Ls[0], t)
            t = copy_act(AT[:, 0:i + 1, i * P:i * P + P], bank[:, 0:n].rearrange("p (j q) -> p j q", j=i + 1), t, atf)
            misc.give(bank, t)
            t_at.append(t)
            yield
        kp.give(k, t_at)
        tbp.give(tb, t_at)
        bank, bf = misc.take()
        for j in range(NT):
            t = mm(bank[:, j * P:S], V[:, j, h * P:h * P + P], AT[:, j, j * P:S], bf, t_at, t_v, start=j == 0,
                   stop=j == NT - 1)
        ATp.give(AT, t)
        ob, of = Op.take()
        t = copy_dve(ob[:, :], bank[:, :], t, of)
        misc.give(bank, t)
        sq, fr = sq_pool.take()
        t_s = func(ACT.Square, sq[:, :], ob[:, :], t, fr)
        rq, rf = rqp.take()
        t8, tf = sm.take()
        yield
        t_r, _ = inv_rms(sq, [t_s, tf], 1.0 / P, rq, rf, tok_out=t8[:, 0:4])
        sm.give(t8, t_r)
        sq_pool.give(sq, t_r)
        t = stt(ob[:, :], ob[:, :], sbl[:, 0:1], rq[:, :], MUL, MUL, t_r, t_sb)
        rqp.give(rq, t)
        hh, ll = XAh[:, h, :], XAl[:, h, :]
        t_h = copy_act(hh, ob[:, :], t, t_qlast)
        t_l = tt(ll, ob[:, :], hh.bitcast(F), SUB, t_h, t_qlast)
        Op.give(ob, t_l)
        o_out.append((hh, ll, t_l))
        yield

    diff_bias(0)
    diff_k(0)
    for h in range(8):
        if h < 7:
            diff_bias(h + 1)
            weave([lambda: diff_k(h + 1)], diff_head(h), 4)
        else:
            weave([], diff_head(h))
    n_f1 = Norm("ffn_ln1", XBh, XBl, [Q.last["pe"]])
    for c in range(DC):
        bank, bf = main.take()
        t = proj(bank[:, :], "attn_out", c * P, o_out, DC, bf)
        x_tok[c] = [add_to_x(c, bank, t, x_tok[c])]
        norm_post(n_f1)(c)
    rows = n_f1.finish()
    C.close()
    check_stop("attn")
    nm = Norm("mix", XAh, XAl, None)
    run_ffn("up1", 0, "up1", 2816, "down1", n_f1.X, rows, ("fcw1", "fcb1"), nm)
    rows = nm.finish()
    check_stop("ffn1")

    G = ExitStack()
    before = Q.ends()
    t_row, t_tok = rows
    X = nm.X
    s_sp = Slot(sem("s_spill"))
    t_spill = Q.dma("act", lambda e: e.dma_start(dram["spill"].rearrange("(c p) n -> p c n", p=P), x[:, :, :]), s_sp, x_tok)
    part = x
    Qb, Kb, Vb = sb(G, [P, 4, S]), sb(G, [P, 4, S]), sb(G, [P, NT, 512])
    MGh, MGl = sb(G, [P, 4, S], R), sb(G, [P, 4, S], R)
    us = [sb(G, [P, S + 4]) for _ in range(1)]
    t_pad = [memset(u[:, 0:4], 0.0, before) for u in us]
    u_pool = Pool(us, t_pad, before)
    vp = Pool([sb(G, [P, S]) for _ in range(3)], before)
    Lp = Pool([sb(G, [P, S]) for _ in range(3)], before)
    ATp = Pool([sb(G, [P, NT, S]) for _ in range(1)], before)
    ckp = Pool([sb(G, [P, S]) for _ in range(2)], before)
    sm = Pool([sb(G, [P, 8]) for _ in range(6)], before)
    cfs, nc_ = sb(G, [P, 32]), sb(G, [P, 32])
    cT = sb(G, [8, S])
    nsink = sb(G, [P, 8])
    rt = sb(G, [P, 4])
    tb2 = Pool([sb(G, [P, 256]) for _ in range(2)], before)
    s_tb2 = [Slot(sem(f"s_tb2{i}")) for i in range(2)]
    t_ns = ts(nsink[:, :], pc("sink", 0, 8), -1.0, None, MUL, None, before)
    t_rt = copy_dve(rt[:, :], rstok[:, 0:4], t_tok, before)
    xb_free = flat([before])

    bank, bf = main.take()
    u, wh, wl, tw = W.unit("w_in", 0, 8, 3072, 8)
    for j in range(NT):
        for c in range(DC):
            a = slice(j * P, j * P + P)
            o_ = bank[:, 8 * j:8 * j + 8]
            mm(o_, X[c][0][:, a], wl[:, c, :], tw, X[c][2], bf, start=c == 0, stop=False)
            mm(o_, X[c][1][:, a], wh[:, c, :], start=False, stop=False)
            t = mm(o_, X[c][0][:, a], wh[:, c, :], start=False, stop=c == DC - 1)
    W.done(u, t)
    for j in range(NT):
        b = slice(8 * j, 8 * j + 8)
        t = stt(cfs[:, b], bank[:, b], rt[:, j:j + 1], pc("fbias", 0, 8), MUL, ADD, t, t_rt, before)
    main.give(bank, t)
    t = ts(nc_[:, :], cfs[:, :], -1.0, None, MUL, None, t, before)
    t = tt(nc_[:, :], nc_[:, :], cfs[:, :], MIN, t)
    t = func(ACT.Exp, nc_[:, :], nc_[:, :], t)
    t = func(ACT.Ln, nc_[:, :], nc_[:, :], t, bias=1.0)
    t_lf = stt(cfs[:, :], cfs[:, :], 0.0, nc_[:, :], MIN, SUB, t)
    bank, bf = misc.take()
    for j in range(NT):
        for i in range(j + 1):
            t = mm(bank[:, 8 * j:8 * j + 8], tri if i == j else ones, cfs[:, 8 * i:8 * i + 8], t_lf, bf,
                   start=i == 0, stop=i == j)
    t_c = copy_dve(cfs[:, :], bank[:, 0:32], t)
    t_nc = ts(nc_[:, :], cfs[:, :], -1.0, None, MUL, None, t_c, t_lf)
    misc.give(bank, t_c)
    bank, bf = misc.take()
    for j in range(NT):
        t = turn(bank[0:8, j * P:j * P + P], cfs[:, 8 * j:8 * j + 8], bf, t_c)
    t_cT = copy_act(cT[:, :], bank[0:8, :], t, before)
    misc.give(bank, t_cT)

    def scaled(name_col, dst, free, scale, nm_="w_in"):
        bank, bf = main.take()
        t = proj(bank[:, :], nm_, name_col, X, DC, bf)
        t1 = stt(dst, bank[:, :], scale, rsrow[:, :], MUL, MUL, t, t_row, free)
        main.give(bank, t1)
        leave_rows(t1)
        return t1

    def conv_tile(i):
        zb, zf = u_pool.take()
        v, vf = vp.take()
        t_c = scaled(512 + i * P, v[:, :], vf, 1.0)
        bank, bf = main.take()
        t = proj(bank[:, :], "w_in", 1024 + i * P, X, DC, bf)
        t1 = tt(zb[:, 4:S + 4], bank[:, :], rsrow[:, :], MUL, t, t_row, zf)
        main.give(bank, t1)
        leave_rows(t1)
        t1 = tt(zb[:, 4:S + 4], zb[:, 4:S + 4], v[:, :], MUL, t1, t_c)
        t = copy_act(v[:, :], zb[:, 2:S + 2], t1, scale=pc("cw2", 3 * i))
        for k in (1, 2):
            t = stt(v[:, :], zb[:, 2 + k:S + 2 + k], pc("cw2", 3 * i + k), v[:, :], MUL, ADD, t)
        u_pool.give(zb, t)
        w, wf = vp.take()
        t_b = scaled(i * P, w[:, :], wf, 1.0)
        t = tt(w[:, :], w[:, :], v[:, :], MUL, t, t_b)
        vp.give(v, t)
        h, lo = XBh[:, 4 + i, :], XBl[:, 4 + i, :]
        t_h = copy_act(h, w[:, :], t, xb_free)
        t_l = tt(lo, w[:, :], h.bitcast(F), SUB, t_h, xb_free)
        vp.give(w, t_l)
        st["Yc"].append((h, lo, t_l))

    t_part = [[t_spill] for _ in range(DC)]

    def branch_tile(i, Yname, c, last=False):
        Y = st[Yname]
        v, vf = vp.take()
        t = scaled(3848 + i * D + c * P, v[:, :], vf, 1.0)
        t_g = func(ACT.Sigmoid, v[:, :], v[:, :], t)
        bank, bf = main.take()
        t = proj(bank[:, :], f"branch{i}", c * P, Y, 4, bf, per=4)
        t_m = tt(v[:, :], bank[:, :], v[:, :], MUL, t, t_g)
        main.give(bank, t_m)
        if i == 0:
            t_p = op("pool", lambda e: e.tensor_copy(part[:, c, :], v[:, :]), t_m, t_part[c])
            vp.give(v, t_p)
            t_part[c] = [t_p]
        elif not last:
            t_p = tt(part[:, c, :], part[:, c, :], v[:, :], ADD, t_m, t_part[c], eng="pool")
            vp.give(v, t_p)
            t_part[c] = [t_p]
        else:
            t_p = tt(v[:, :], part[:, c, :], v[:, :], ADD, t_m, t_part[c])
            t_part[c] = [t_p]
            h, lo = (XBh[:, c, :], XBl[:, c, :]) if c < 4 else (MGh[:, c - 4, :], MGl[:, c - 4, :])
            t_h = copy_act(h, v[:, :], t_p, st["mg_free"])
            t_l = tt(lo, v[:, :], h.bitcast(F), SUB, t_h, st["mg_free"])
            vp.give(v, t_l)
            st["mg"].append((h, lo, t_l))
        return t

    def soft_out(Ls, s8, n, t_den, AT, atf, dst, *w):
        t = recip(s8[:, 5:6], s8[:, 4:5], t_den)
        t_a = ts(Ls[:, 0:n], Ls[:, 0:n], s8[:, 5:6], None, MUL, None, t)
        sm.give(s8, t_a)
        bank, bf = misc.take()
        for j in range(n // P):
            t = turn(bank[:, j * P:j * P + P], Ls[:, j * P:j * P + P], t_a, bf)
        Lp.give(Ls, t)
        t = copy_act(dst, bank[:, 0:n].rearrange("p (j q) -> p j q", j=n // P), t, atf)
        misc.give(bank, t)
        return t

    def fin_pair(bank, t, ch, name, free):
        h, lo = XBh[:, ch, :], XBl[:, ch, :]
        t_h = copy_act(h, bank[:, :], t, free)
        t_l = tt(lo, bank[:, :], h.bitcast(F), SUB, t_h, free)
        misc.give(bank, t_l)
        st[name].append((h, lo, t_l))

    def swa_bias(h):
        tb, tbf = tb2.take()

        def get(e):
            flat_ = dram["tab2"][h].rearrange("p n -> (p n)")
            return e.dma_start(tb[:, :], flat_[127:127 + P * (L2 - 1)].rearrange("(p n) -> p n", n=L2 - 1)[:, 0:256])

        st["tb2", h] = (tb, Q.dma("act", get, s_tb2[st["n2"] % 2], tbf, t_tabs))
        st["n2"] += 1

    def swa(tile):
        ob, obf = misc.take()
        for half in range(2):
            h = tile + 4 * half
            swa_bias(h)
            tb, t_tb = st["tb2", h]
            r = slice(64 * half, 64 * half + 64)
            AT, atf = ATp.take()
            t_at = []
            for i in range(NT):
                a0 = max(i - 1, 0) * P
                n = (i + 1) * P - a0
                bank, bf = misc.take()
                t = mm(bank[:, 0:n], Qb[r, tile, i * P:i * P + P], Kb[r, 0, a0:a0 + n], bf, st["sq"][tile], st["sk"])
                lb, lf = Lp.take()
                s8, sf = sm.take()
                t = add_min(lb[:, 0:n], bank[:, 0:n], tb[:, 256 - n:256], s8[:, 0:1], t, t_tb, lf, sf)
                misc.give(bank, t)
                t = tt(s8[:, 1:2], s8[:, 0:1], nsink[:, h:h + 1], MIN, t, t_ns)
                t_e = func(ACT.Exp, lb[:, 0:n], lb[:, 0:n], t, bias=s8[:, 1:2], scale=-1.0, accum=s8[:, 2:3])
                t_s = func(ACT.Exp, s8[:, 3:4], s8[:, 1:2], t, bias=pc("sink", h), scale=1.0)
                t = tt(s8[:, 4:5], s8[:, 2:3], s8[:, 3:4], ADD, t_e, t_s)
                yield
                dst = AT[:, 0:n // P, i * P:i * P + P]
                t_at.append(soft_out(lb, s8, n, t, AT, atf, dst))
                yield
            tb2.give(tb, t_at)
            for i in range(NT):
                js = [i] if i == 0 else [i - 1, i]
                for m_, j in enumerate(js):
                    t = mm(ob[64 * half:64 * half + 64, i * P:i * P + P], Vb[:, j, 64 * half:64 * half + 64],
                           AT[:, m_, i * P:i * P + P], obf, t_at, st["sv"], start=m_ == 0, stop=m_ == len(js) - 1)
            ATp.give(AT, t)
            yield
        fin_pair(ob, t, tile, "Ys", xb_free)
        yield

    def fox(tile):
        ob, obf = misc.take()
        for half in range(2):
            h = 2 * tile + half
            r = slice(64 * half, 64 * half + 64)
            bank, bf = misc.take()
            t = mm(bank[:, :], ident[0:8, h:h + 1].to_broadcast([8, P]), cT[:, :], bf, t_cT)
            ck, ckf = ckp.take()
            t_ck = copy_act(ck[:, :], bank[:, :], t, ckf)
            misc.give(bank, t_ck)
            AT, atf = ATp.take()
            t_at, t_cks = [], []
            yield
            for i in range(NT):
                n = (i + 1) * P
                cki, cf = ckp.take()
                t_ci = ts(cki[:, 0:n], ck[:, 0:n], nc_[:, 8 * i + h:8 * i + h + 1], 1.0, ADD, MUL, t_ck, t_nc, cf, eng="pool")
                bank, bf = misc.take()
                mm(bank[:, 0:n], Qb[r, tile, i * P:i * P + P], Kb[r, tile, 0:n], bf, st["fq"][tile], st["fk"][tile], stop=False)
                t = mm(bank[:, i * P:n], identb[:, :], maskb[:, 0, :], start=False)
                lb, lf = Lp.take()
                s8, sf = sm.take()
                t = add_min(lb[:, 0:n], bank[:, 0:n], cki[:, 0:n], s8[:, 0:1], t, t_ci, lf, sf)
                misc.give(bank, t)
                ckp.give(cki, t)
                t_e = func(ACT.Exp, lb[:, 0:n], lb[:, 0:n], t, bias=s8[:, 0:1], scale=-1.0, accum=s8[:, 4:5])
                t_cks.append(t_ci)
                yield
                t_at.append(soft_out(lb, s8, n, t_e, AT, atf, AT[:, 0:i + 1, i * P:i * P + P]))
                yield
            ckp.give(ck, t_cks)
            for j in range(NT):
                t = mm(ob[64 * half:64 * half + 64, j * P:S], Vb[:, j, 64 * h:64 * h + 64], AT[:, j, j * P:S], obf, t_at,
                       st["fv"], start=j == 0, stop=j == NT - 1)
            ATp.give(AT, t)
            yield
        fin_pair(ob, t, 4 + tile, "Yf", st["yf_free"])
        yield

    st["n2"] = 0
    st["Yc"], st["Ys"], st["Yf"], st["mg"] = [], [], [], []
    st["sq"] = [scaled(("swaq", i), Qb[:, i, :], before, -0.125) for i in range(4)]
    st["sk"] = scaled(3080 + 512, Kb[:, 0, :], before, 1.0)
    bk = [misc.take() for _ in range(NT)]
    ts_ = proj_tok([b[:, 0:P] for b, _ in bk], "w_in", 3080 + 640, P, X, DC, 8, [f for _, f in bk])
    st["sv"] = []
    for j in range(NT):
        t = copy_act(Vb[:, j, 0:P], bk[j][0][:, 0:P], ts_[j], t_rt, before, scale=rt[:, j:j + 1])
        misc.give(bk[j][0], t)
        st["sv"].append(t)
    jobs = [lambda i=i: conv_tile(i) for i in range(4)] + [lambda c=c: branch_tile(0, "Yc", c) for c in range(DC)]
    weave(jobs, chain(*[swa(t) for t in range(4)]), 6)
    free_q = Q.ends()
    st["yf_free"] = free_q
    st["fq"] = [scaled(1536 + i * P, Qb[:, i, :], free_q, -0.125) for i in range(4)]
    st["fk"] = [scaled(2048 + i * P, Kb[:, i, :], free_q, 1.0) for i in range(4)]
    bk = [misc.take() for _ in range(NT)]
    ts_ = proj_tok([b[:, :] for b, _ in bk], "w_in", 2560, 512, X, DC, 2, [f for _, f in bk])
    st["fv"] = []
    for j in range(NT):
        t = copy_act(Vb[:, j, :], bk[j][0][:, :], ts_[j], t_rt, free_q, scale=rt[:, j:j + 1])
        misc.give(bk[j][0], t)
        st["fv"].append(t)
    jobs = [lambda c=c: branch_tile(2, "Ys", c) for c in range(DC)]
    weave(jobs, chain(*[fox(t) for t in range(4)]), 11)
    st["mg_free"] = [Q.last["pe"], before]
    for c in range(DC):
        branch_tile(1, "Yf", c, last=True)
    s_re = Slot(sem("s_reload"))
    t_re = Q.dma("act", lambda e: e.dma_start(x[:, :, :], dram["spill"].rearrange("(c p) n -> p c n", p=P)), s_re,
                 t_part, t_spill)
    for c in range(DC):
        x_tok[c] = [t_re]
    G.close()
    nx = Norm("xattn", XAh, XAl, [Q.last["pe"]])
    for c in range(DC):
        bank, bf = main.take()
        t = proj(bank[:, :], "mix_out", c * P, st["mg"], DC, bf)
        x_tok[c] = [add_to_x(c, bank, t, x_tok[c])]
        norm_post(nx)(c)
    mix_end = Q.ends()
    rows = nx.finish()
    check_stop("mix")

    G = ExitStack()
    before = [Q.ends(), mix_end]
    t_row, t_tok = rows
    M = 256
    mem = sb(G, [P, DC, M])
    mh, ml = sb(G, [P, DC, M], R), sb(G, [P, DC, M], R)
    macc, msq = sb(G, [P, M]), sb(G, [P, M])
    mrow = sb(G, [P, M])
    mtok = sb(G, [P, 4])
    Kx, Vx = sb(G, [P, DC, M]), sb(G, [P, 2, D])
    qp = Pool([sb(G, [P, 2, S]) for _ in range(2)], before)
    Lp = Pool([sb(G, [P, S]) for _ in range(3)], before)
    ATp = Pool([sb(G, [P, NT, S]) for _ in range(1)], before)
    sm = Pool([sb(G, [P, 8]) for _ in range(6)], before)
    s_mem = Slot(sem("s_mem"))
    t_mem = Q.dma("act", lambda e: e.dma_start(mem[:, :, :], dram["mem"].rearrange("(c p) n -> p c n", p=P)), s_mem, before)
    MX, t_a = [], None
    for c in range(DC):
        g = pc("mem", c)
        t_h = copy_act(mh[:, c, :], mem[:, c, :], t_mem, before, scale=g)
        t_l = stt(ml[:, c, :], mem[:, c, :], g, mh[:, c, :].bitcast(F), MUL, SUB, t_h, before)
        MX.append((mh[:, c, :], ml[:, c, :], t_l))
        if c == 0:
            t_a = func(ACT.Square, macc[:, :], mem[:, c, :], t_mem, before)
        else:
            t_s = func(ACT.Square, msq[:, :], mem[:, c, :], t_mem, before, t_a)
            t_a = tt(macc[:, :], macc[:, :], msq[:, :], ADD, t_s, t_a, eng="pool")
    t_mrow, t_mt = inv_rms(macc, t_a, 1.0 / D, mrow, before, width=M, tok_out=mtok[:, 0:2])
    t_kx = []
    for c in range(DC):
        bank, bf = main.take()
        t = proj(bank[:, 0:M], "xkv", c * P, MX, DC, bf)
        t = tt(Kx[:, c, :], bank[:, 0:M], mrow[:, :], MUL, t, t_mrow, before)
        main.give(bank, t)
        t_kx.append(t)
    t_vx = []
    for half in range(2):
        bk = [misc.take() for _ in range(2)]
        ts_ = proj_tok([b[:, :] for b, _ in bk], "xkv", D + 512 * half, 512, MX, DC, 2, [f for _, f in bk])
        for j in range(2):
            t = copy_act(Vx[:, j, 512 * half:512 * half + 512], bk[j][0][:, :], ts_[j], t_mt, before,
                         scale=mtok[:, j:j + 1])
            misc.give(bk[j][0], t)
            t_vx.append(t)

    def xq(h):
        qb, qf = qp.take()
        tq = []
        for i in range(2):
            bank, bf = main.take()
            t = proj(bank[:, :], "xq", (2 * h + i) * P, nx.X, DC, bf)
            t1 = stt(qb[:, i, :], bank[:, :], -1.0 / 16, rsrow[:, :], MUL, MUL, t, t_row, qf)
            main.give(bank, t1)
            leave_rows(t1)
            tq.append(t1)
        st["xq", h] = (qb, tq)

    OX = [None] * DC

    def xhead(h):
        qb, tq = st["xq", h]
        AT, atf = ATp.take()
        t_at = []
        for i in range(NT):
            bank, bf = misc.take()
            for d in range(2):
                t = mm(bank[:, 0:M], qb[:, d, i * P:i * P + P], Kx[:, 2 * h + d, :], bf, tq, t_kx, start=d == 0, stop=d == 1)
            lb, lf = Lp.take()
            s8, sf = sm.take()
            t = op("dve", lambda e, s8=s8, bank=bank: e.tensor_reduce(s8[:, 0:1], bank[:, 0:M], mybir.AxisListType.X, MIN), t, sf)
            t = func(ACT.Exp, lb[:, 0:M], bank[:, 0:M], t, lf, bias=s8[:, 0:1], scale=-1.0, accum=s8[:, 4:5])
            misc.give(bank, t)
            yield
            t_at.append(soft_out(lb, s8, M, t, AT, atf, AT[:, 0:2, i * P:i * P + P]))
            yield
        qp.give(qb, t_at)
        for d in range(2):
            bank, bf = misc.take()
            for j in range(2):
                t = mm(bank[:, :], Vx[:, j, h * 256 + d * P:h * 256 + d * P + P], AT[:, j, :], bf, t_at, t_vx,
                       start=j == 0, stop=j == 1)
            ch = 2 * h + d
            hh, ll = XBh[:, ch, :], XBl[:, ch, :]
            t_h = copy_act(hh, bank[:, :], t, mix_end)
            t_l = tt(ll, bank[:, :], hh.bitcast(F), SUB, t_h, mix_end)
            misc.give(bank, t_l)
            OX[ch] = (hh, ll, t_l)
            yield
        ATp.give(AT, t)

    xq(0)
    for h in range(4):
        weave([lambda: xq(h + 1)] if h < 3 else [], xhead(h), 2)
    n2 = Norm("ffn2", XAh, XAl, [Q.last["pe"]])
    for c in range(DC):
        bank, bf = main.take()
        t = proj(bank[:, :], "xo", c * P, OX, DC, bf)
        x_tok[c] = [add_to_x(c, bank, t, x_tok[c])]
        norm_post(n2)(c)
    rows = n2.finish()
    G.close()
    check_stop("xattn")

    nl = {"t": None}

    def last(c):
        sq, fr = sq_pool.take()
        t_x = x_tok[c]
        if c == 0:
            nl["t"] = t_s = func(ACT.Square, acc[:, :], x[:, c, :], t_x, rs_state["acc"])
            sq_pool.give(sq, fr)
        else:
            t_s = func(ACT.Square, sq[:, :], x[:, c, :], t_x, fr)
            nl["t"] = tt(acc[:, :], acc[:, :], sq[:, :], ADD, t_s, nl["t"], eng="pool")
            sq_pool.give(sq, nl["t"])
        x_tok[c] = x_tok[c] + [t_s]

    ffn("gate2", 0, "up2", 0, "down2", n2.X, rows[0], None, last)
    t_r, _ = inv_rms(acc, nl["t"], 1.0 / D, rsrow, rs_state["row"])
    for c in range(DC):
        t = stt(x[:, c, :], x[:, c, :], pc("final", c), rsrow[:, :], MUL, MUL, t_r, x_tok[c])
        if c % 2:
            Q.dma("sp", lambda e, c=c: e.dma_start(
                dram["out"][(c - 1) * P:(c + 1) * P, :].rearrange("(c p) n -> p c n", p=P), x[:, c - 1:c + 1, :]), s_out, t)
    return Q, W, sems, s_out


def weight_table(a):
    t = {
        "ssm_in": a["ssm_in_w"][0], "ssm_out": a["ssm_out_w"][0], "kv_w": a["kv_w"], "q_w": a["q_w"][0],
        "attn_out": a["attn_out_w"][0], "up0": a["ffn_up_w"][0], "up1": a["ffn_up_w"][1],
        "down0": a["ffn_down_w"][0], "down1": a["ffn_down_w"][1], "w_in": a["w_in_2"][0],
        "mix_out": a["w_mix_out_2"][0], "xq": a["w_xq_2"][0], "xkv": a["w_xkv_2"][0], "xo": a["w_xo_2"][0],
        "gate2": a["w_ffn_gate_2"][0], "up2": a["w_ffn_up_2"][0], "down2": a["w_ffn_down_2"][0],
        "branch0": a["w_branch_2"][0, 0], "branch1": a["w_branch_2"][0, 1], "branch2": a["w_branch_2"][0, 2],
    }
    t = {k: np.asarray(v) for k, v in t.items()}
    t["branch2"] = t["branch2"].reshape(2, 4, 64, D).transpose(1, 0, 2, 3).reshape(512, D)
    return t


def pack(plan, table):
    out = np.empty(plan[-1][-2] + P * plan[-1][-1], np.float32)
    for name, r0, nk, c0, ncol, off, n in plan:
        rows = table[name][r0 * P:(r0 + nk) * P]
        if isinstance(c0, tuple):
            c = 3080 + np.concatenate([np.arange(64) + 64 * c0[1], np.arange(64) + 64 * (c0[1] + 4)])
            b = rows[:, c]
        else:
            b = rows[:, c0:c0 + ncol]
        out[off:off + P * n] = b.reshape(nk, P, ncol).transpose(1, 0, 2).reshape(-1)
    return out


def build(nc, scratch, mk, stop=None):
    with ExitStack() as ctx:
        _, W, _, _ = emit_safe(scratch, ctx, None, {}, stop)
    plan, off = [], 0
    for w in W.want:
        n = w[2] * w[4]
        plan.append((*w, off, n))
        off += P * n
    dram = mk(off)
    with ExitStack() as ctx:
        Q, _, sems, s_out = emit_safe(nc, ctx, plan, dram, stop)
        Q.number(sems)
        block = ctx.enter_context(nc.Block())

        @block.tensor
        def _(e):
            Q.play("pe", e)

        @block.scalar
        def _(e):
            Q.play("act", e)

        @block.vector
        def _(e):
            Q.play("dve", e)

        @block.gpsimd
        def _(e):
            Q.play("pool", e)

        @block.sync
        def _(e):
            Q.play("sp", e)
            e.wait_ge(s_out.sem, 16 * s_out.n)

    return plan


def emit_safe(nc, ctx, plan, dram, stop):
    try:
        return emit(nc, ctx, plan, dram, stop)
    except Stop as e:
        return e.args


def kernel(**inputs):
    import concourse.bacc as _bacc
    from concourse.bass_utils import run_bass_kernel_spmd as _run

    a = {k: np.asarray(v) for k, v in inputs.items()}
    nc = _bacc.Bacc("TRN2", target_bir_lowering=False, num_devices=1)
    scratch = _bacc.Bacc("TRN2", target_bir_lowering=False, num_devices=1)
    keep, once = constants()
    arrays = {
        "x": np.ascontiguousarray(a["x"][0].T), "mem": np.ascontiguousarray(a["mem_2"][0].T),
        "par": parameters(a), "keep": keep, "once": once,
    }

    def mk(n):
        dram = {k: nc.dram_tensor(f"in_{k}", v.shape, F, kind="ExternalInput").ap() for k, v in arrays.items()}
        dram["w"] = nc.dram_tensor("in_w", (n,), F, kind="ExternalInput").ap()
        dram["out"] = nc.dram_tensor("out_0", (D, S), F, kind="ExternalOutput").ap()
        dram["tab1"] = nc.dram_tensor("tab1", (8, P, L1), F).ap()
        dram["tab2"] = nc.dram_tensor("tab2", (8, P, L2), F).ap()
        dram["spill"] = nc.dram_tensor("spill", (D, S), F).ap()
        return dram

    plan = build(nc, scratch, mk)
    ins = {f"in_{k}": v for k, v in arrays.items()}
    ins["in_w"] = pack(plan, weight_table(a))
    r = _run(nc, [ins], core_ids=[0])
    return np.ascontiguousarray(r.results[0]["out_0"].T)[None]
```

```python
from contextlib import ExitStack

import numpy as np

import concourse.bass as bass
from concourse import mybir

F = mybir.dt.float32
R = mybir.dt.float32r
BF = mybir.dt.bfloat16
ALU = mybir.AluOpType
ACT = mybir.ActivationFunctionType
MUL, ADD, SUB, MIN, MAX, POW = ALU.mult, ALU.add, ALU.subtract, ALU.min, ALU.max, ALU.pow

P = 128
S = 512
D = 1024
DC = D // P
NT = S // P
EPS = 1e-6
LAM_INIT = 0.8 - 0.6 * float(np.exp(-0.3))
FFC = 22
BIG = 1e30
FMAX = 3.0e38
ENGINES = ("pe", "act", "dve", "pool", "sp")

N_RAW, N_W, AHEAD = 3, 3, 2
UNIT = 1024


class Tok:

    def __init__(self, eng):
        self.eng, self.used, self.sem, self.val = eng, False, None, 0


class Slot:

    def __init__(self, sem):
        self.sem, self.n = sem, 0


def flat(x):
    if x is None:
        return []
    if isinstance(x, Tok):
        return [x]
    return [t for y in x for t in flat(y)]


class Queues:
    def __init__(self):
        self.q = {e: [] for e in ENGINES}
        self.last = {}

    def op(self, eng, fn, *waits):
        w = flat(waits)
        for t in w:
            t.used = True
        tok = Tok(eng)
        self.q[eng].append((fn, w, tok))
        self.last[eng] = tok
        return tok

    def dma(self, eng, fn, slot, *waits):
        w = flat(waits)
        for t in w:
            t.used = True
        tok = Tok("dma")
        slot.n += 1
        tok.sem, tok.val = slot.sem, 16 * slot.n
        self.q[eng].append((fn, w, tok))
        return tok

    def ends(self):
        return [self.last[e] for e in ("pe", "act", "dve", "pool") if e in self.last]

    def number(self, sems):
        for e in ENGINES:
            n = 0
            for _, _, tok in self.q[e]:
                if tok.eng != "dma" and tok.used:
                    n += 1
                    tok.sem, tok.val = sems[e], n

    def play(self, name, eng):
        seen = {}
        for fn, waits, tok in self.q[name]:
            need = {}
            for t in waits:
                k = id(t.sem)
                if t.val > need.get(k, (None, 0))[1]:
                    need[k] = (t.sem, t.val)
            for k, (sem, val) in need.items():
                if seen.get(k, 0) < val:
                    eng.wait_ge(sem, val)
                    seen[k] = val
            ins = fn(eng)
            if tok.eng == "dma":
                ins.then_inc(tok.sem, 16)
            elif tok.used:
                ins.then_inc(tok.sem, 1)


class Pool:

    def __init__(self, bufs, *after):
        self.free = [(b, flat(after)) for b in bufs]

    def take(self):
        return self.free.pop(0)

    def give(self, buf, *toks):
        self.free.append((buf, flat(toks)))


def t5_bucket(n):
    n = np.maximum(n, 0)
    big = np.maximum(n, 1).astype(np.float32)
    large = 16 + (np.log(big / np.float32(16)) / np.float32(np.log(8.0)) * np.float32(16)).astype(np.int32)
    return np.where(n < 16, n, np.minimum(large, 31))


L1, L2 = 640, 384


def constants():
    i = np.arange(P)
    ident = np.eye(P, dtype=np.float32)
    tri = (i[:, None] <= i[None, :]).astype(np.float32)
    above = np.where(i[None, :] > i[:, None], BIG, 0).astype(np.float32)
    blk = np.zeros((P, 2), np.float32)
    blk[:64, 0] = blk[64:, 1] = 1
    d1, d2 = 511 - np.arange(L1), 255 - np.arange(L2)
    oh1, oh2 = np.zeros((P, L1), np.float32), np.zeros((P, L2), np.float32)
    ok1, ok2 = d1 >= 0, (d2 >= 0) & (d2 < 128)
    oh1[t5_bucket(d1)[ok1], np.arange(L1)[ok1]] = 1
    oh2[t5_bucket(d2)[ok2], np.arange(L2)[ok2]] = 1
    m1 = np.tile(np.where(ok1, 0, BIG).astype(np.float32), (P, 1))
    m2 = np.tile(np.where(ok2, 0, BIG).astype(np.float32), (P, 1))
    keep = np.concatenate([ident, tri, np.ones((P, P), np.float32), blk, above], 1)
    once = np.concatenate([oh1, m1, oh2, m2], 1)
    return keep, once


N_KEEP = 4 * P + 2
N_ONCE = 2 * L1 + 2 * L2

PAR = {}


def _lay():
    at = 0
    for name, n in [
        ("ssm_ln", 8), ("kv_ln", 8), ("attn_ln", 8), ("ffn_ln0", 8), ("ffn_ln1", 8), ("mix", 8), ("xattn", 8),
        ("mem", 8), ("ffn2", 8), ("final", 8), ("scw", 96), ("scb", 24), ("sng", 16), ("sd", 16), ("dtb", 32),
        ("alog", 32), ("kn", 1), ("qn", 1), ("lam", 256), ("subln", 1), ("rel", 8), ("rel2", 8), ("fcw0", 132),
        ("fcb0", 44), ("fcw1", 132), ("fcb1", 44), ("fbias", 8), ("cw2", 12), ("sink", 8),
    ]:
        PAR[name] = (at, n)
        at += n
    return at


N_PAR = _lay()


def cols(v):
    return np.asarray(v).reshape(-1, P).T


def parameters(a):
    def rows(v):
        return np.broadcast_to(np.asarray(v).reshape(1, -1), (P, np.asarray(v).size))

    def taps(w):
        w = np.asarray(w)
        return w.reshape(w.shape[0], -1, P).transpose(2, 1, 0).reshape(P, -1)

    def table(v):
        out = np.zeros((P, 8), np.float32)
        out[:32] = v
        return out

    got = {
        "ssm_ln": cols(a["ssm_ln_g"]), "kv_ln": cols(a["kv_ln_g"]), "attn_ln": cols(a["attn_ln_g"]),
        "ffn_ln0": cols(a["ffn_ln_g"][0]), "ffn_ln1": cols(a["ffn_ln_g"][1]), "mix": cols(a["mix_norm_g_2"]),
        "xattn": cols(a["xattn_norm_g_2"]), "mem": cols(a["mem_norm_g_2"]), "ffn2": cols(a["ffn_norm_g_2"]),
        "final": cols(a["final_norm_g_2"]), "scw": taps(a["ssm_conv_w"][0]), "scb": cols(a["ssm_conv_b"]),
        "sng": cols(a["ssm_norm_g"]), "sd": cols(np.repeat(np.asarray(a["ssm_d"])[0], 64)),
        "dtb": rows(a["ssm_dt_bias"]), "alog": rows(a["ssm_a_log"]),
        "kn": cols(np.tile(a["k_norm_g"], 2)), "qn": cols(np.tile(np.asarray(a["q_norm_g"])[0], 2)),
        "lam": rows(a["lam_vecs"]), "subln": cols(a["subln_g"]), "rel": table(a["rel_bias"]),
        "rel2": table(a["rel_bias_2"]), "fcw0": taps(a["ffn_conv_w"][0]), "fcb0": cols(a["ffn_conv_b"][0]),
        "fcw1": taps(a["ffn_conv_w"][1]), "fcb1": cols(a["ffn_conv_b"][1]), "fbias": rows(a["forget_bias_2"]),
        "cw2": taps(a["conv_w_2"][0]), "sink": rows(a["sink_2"]),
    }
    return np.concatenate([got[k] for k in PAR], 1).astype(np.float32)


def emit(nc, ctx, plan, dram):
    Q = Queues()
    op = Q.op
    names = [0]

    def sb(scope, shape, dt=F, side="left"):
        names[0] += 1
        return scope.enter_context(nc.sbuf_tensor(f"t{names[0]}", shape, dt, side=side))

    def sem(name):
        return ctx.enter_context(nc.semaphore(name))

    sems = {e: sem(f"done_{e}") for e in ENGINES}

    x = sb(ctx, [P, DC, S])
    XAh, XAl = sb(ctx, [P, DC, S], R), sb(ctx, [P, DC, S], R)
    keep = sb(ctx, [P, N_KEEP])
    par = sb(ctx, [P, N_PAR])
    maskb = sb(ctx, [P, P], BF)
    identr = sb(ctx, [32, 32], R)
    identb = sb(ctx, [P, P], BF)
    mhalf = sb(ctx, [P, 8])
    rsrow = sb(ctx, [P, S])
    acc = sb(ctx, [P, S])
    sqs = [sb(ctx, [P, S]) for _ in range(2)]
    stat = sb(ctx, [P, 4, 8])
    rstok = sb(ctx, [P, 8])
    raws = [sb(ctx, [P, UNIT]) for _ in range(N_RAW)]
    his = [sb(ctx, [P, UNIT], R) for _ in range(N_W)]
    los = [sb(ctx, [P, UNIT], R) for _ in range(N_W)]
    banks = [ctx.enter_context(nc.psum_tensor(f"bank{i}", [P, S], F)) for i in range(8)]
    ident, tri, ones = keep[:, 0:P], keep[:, P:2 * P], keep[:, 2 * P:3 * P]
    blk = keep[:, 3 * P:3 * P + 2]

    def pc(name, i=0, n=1):
        return par[:, PAR[name][0] + i:PAR[name][0] + i + n]

    main, misc = Pool(banks[0:3]), Pool(banks[3:8])
    sq_pool = Pool(sqs)

    def copy_act(out, in_, *w, scale=1.0):
        return op("act", lambda e: e.activation(out, in_, ACT.Copy, scale=scale), *w)

    def func(f, out, in_, *w, bias=0.0, scale=1.0, accum=None):
        return op("act", lambda e: e.activation(out, in_, f, bias=bias, scale=scale, accum_out=accum), *w)

    def tt(out, a, b, o, *w, eng="dve"):
        return op(eng, lambda e: e.tensor_tensor(out, a, b, o), *w)

    def stt(out, a, s, b, o0, o1, *w):
        return op("dve", lambda e: e.scalar_tensor_tensor(out=out, in0=a, scalar=s, in1=b, op0=o0, op1=o1), *w)

    def ts(out, a, s0, s1, o0, o1, *w, eng="dve"):
        if o1 is None:
            return op(eng, lambda e: e.tensor_scalar(out, a, s0, None, o0), *w)
        return op(eng, lambda e: e.tensor_scalar(out, a, s0, s1, o0, o1), *w)

    def recip(out, a, *w):
        return op("dve", lambda e: e.reciprocal(out, a), *w)

    def copy_dve(out, in_, *w):
        return op("dve", lambda e: e.tensor_copy(out, in_), *w)

    def add_min(out, a, b, m, *w):
        return op("dve", lambda e: e.tensor_tensor_reduce(out, a, b, 1.0, FMAX, ADD, MIN, m), *w)

    def mm(out, lhs, rhs, *w, start=True, stop=True, loose=False):
        return op("pe", lambda e: e.matmul(out, lhs, rhs, start=start, stop=stop, skip_group_check=loose), *w)

    def turn(out, in_, *w):
        n = in_.shape[0]
        return op("pe", lambda e: e.transpose(out, in_, ident[0:n, 0:n]), *w)

    def memset(out, v, *w):
        return op("pool", lambda e: e.memset(out, v), *w)

    class Weights:
        def __init__(self):
            self.want, self.u = [], 0
            self.loaded = self.split_ = 0
            self.slots = [Slot(sem(f"w{i}")) for i in range(N_RAW)]
            self.arrived, self.cut, self.done_ = {}, {}, {}

        def load(self, v):
            if v >= len(plan):
                return
            off, n = plan[v][-2:]
            dst = raws[v % N_RAW][:, 0:n]

            def go(e):
                src = dram["w"][off:off + P * n].rearrange("(p n) -> p n", p=P)
                return e.dma_start(dst, src)

            self.arrived[v] = Q.dma("sp", go, self.slots[v % N_RAW], self.cut.get(v - N_RAW))

        def split(self, v):
            n = plan[v][-1]
            raw, hi, lo = raws[v % N_RAW][:, 0:n], his[v % N_W][:, 0:n], los[v % N_W][:, 0:n]
            t = copy_act(hi, raw, self.arrived[v], self.done_.get(v - N_W))
            self.cut[v] = tt(lo, raw, hi.bitcast(F), SUB, t, self.done_.get(v - N_W))

        def first(self, n):
            while plan is not None and self.loaded < n:
                self.load(self.loaded)
                self.loaded += 1

        def prepare(self, last):
            if plan is None:
                return
            self.first(N_RAW)
            while self.split_ <= min(last, len(plan) - 1):
                self.split(self.split_)
                self.load(self.loaded)
                self.loaded += 1
                self.split_ += 1

        def unit(self, name, r0, nk, c0, nc_):
            n = nk * nc_
            self.want.append((name, r0, nk, c0, nc_))
            u, self.u = self.u, self.u + 1
            if plan is not None:
                assert plan[u][:5] == (name, r0, nk, c0, nc_)
                self.prepare(u + AHEAD)
            v = (t[u % N_W][:, 0:n].rearrange("p (k n) -> p k n", k=nk) for t in (his, los))
            return u, *v, self.cut.get(u)

        def done(self, u, tok):
            self.done_[u] = tok

    W = Weights()

    class Flow:
        def __init__(self):
            self.live = []

        def start(self, gen, lasting=False, now=False):
            self.live.append((gen, lasting))
            if now:
                self.step(self.live[-1])

        def step(self, item):
            try:
                next(item[0])
            except StopIteration:
                self.live.remove(item)

        def tick(self):
            for item in list(self.live):
                self.step(item)

        def need(self, test):
            n = 0
            while not test():
                self.tick()
                n += 1
                assert n < 5000, "stuck"

        def settle(self):
            self.need(lambda: all(lasting for _, lasting in self.live))

    flow = Flow()

    def take(pool, n=1):
        while len(pool.free) < n:
            yield
        got = [pool.take() for _ in range(n)]
        return got[0] if n == 1 else got

    def grab(pool):
        flow.need(lambda: pool.free)
        return pool.take()

    def operand(X, i):
        flow.need(lambda: X[i] is not None)
        return X[i]

    def proj(out, name, c0, X, nk, *w, per=8, ncol=P, start=True, stop=True):
        tok = None
        for r0 in range(0, nk, per):
            k = min(per, nk - r0)
            u, wh, wl, tw = W.unit(name, r0, k, c0, ncol)
            for c in range(k):
                if c % 2 == 0:
                    flow.tick()
                xh, xl, tx = operand(X, r0 + c)
                first, last = start and r0 + c == 0, stop and r0 + c == nk - 1
                mm(out, wl[:, c, :], xh, tw, tx, w, start=first, stop=False)
                mm(out, wh[:, c, :], xl, start=False, stop=False)
                tok = mm(out, wh[:, c, :], xh, start=False, stop=last)
            W.done(u, tok)
        return tok

    def proj_tok(name, c0, ncol, X, nk, per, nt=NT):
        in_bank = min(nt, S // ncol)
        bk = [grab(main) for _ in range(nt // in_bank)]
        toks = [None] * nt
        for r0 in range(0, nk, per):
            u, wh, wl, tw = W.unit(name, r0, per, c0, ncol)
            for j in range(nt):
                bank, bf = bk[j // in_bank]
                out = bank[:, j % in_bank * ncol:(j % in_bank + 1) * ncol]
                flow.tick()
                for c in range(per):
                    xh, xl, tx = operand(X, r0 + c)
                    a = slice(j * P, j * P + P)
                    mm(out, xh[:, a], wl[:, c, :], tw, tx, bf, start=r0 + c + j % in_bank == 0, stop=False, loose=True)
                    mm(out, xl[:, a], wh[:, c, :], start=False, stop=False, loose=True)
                    toks[j] = mm(out, xh[:, a], wh[:, c, :], start=False, stop=r0 + c == nk - 1, loose=True)
            W.done(u, toks[-1])
        return bk, [(bk[j // in_bank][0][:, j % in_bank * ncol:(j % in_bank + 1) * ncol], toks[-1]) for j in range(nt)]

    def thin(name, c0, ncol, norm, tmp, *w):
        bank, bf = grab(main)
        t = proj(bank[0:ncol, :], name, c0, norm.X, DC, bf, ncol=ncol)
        return thin_steps(bank, ncol, t, norm, tmp, w)

    def thin_steps(bank, ncol, t, norm, tmp, *w):
        while norm.rows is None:
            yield
        t = tt(tmp[0:ncol, :], bank[0:ncol, :], rsrow[0:ncol, :], MUL, t, norm.row(), w)
        main.give(bank, t)
        leave_rows(t)
        return t

    def by_token(tmp, ncol, t):
        bank, bf = yield from take(misc)
        for j in range(NT):
            t_b = turn(bank[:, ncol * j:ncol * j + ncol], tmp[0:ncol, j * P:j * P + P], bf, t)
        yield
        return bank, t_b

    rs_state = {"row": [], "tok": [], "acc": [], "n": 0}
    stat_free = [[] for _ in range(4)]

    def inv_rms(a, t_a, scale, row, row_free, groups=1, width=S, tok_out=None):
        nt, g = width // P, groups
        n = rs_state["n"] % 4
        rs_state["n"] += 1
        bank, free = yield from take(misc)
        rhs = ones[:, 0:1] if g == 1 else blk
        for j in range(nt):
            t = mm(bank[:, j * g:j * g + g], a[:, j * P:j * P + P], rhs, t_a, free)
        yield
        ms = stat[:, n, 0:nt * g]
        dst, t_f = tok_out if tok_out is not None else (ms, None)
        t = ts(ms, bank[:, 0:nt * g], scale, EPS, MUL, ADD, t, stat_free[n])
        t_p = op("pool", lambda e: e.tensor_tensor(dst, ms, mhalf[:, 0:nt * g], POW), t, t_mhalf, t_f)
        for _ in range(3):
            yield
        if g == 1:
            for j in range(nt):
                t = mm(bank[:, j * P:j * P + P], dst[:, j:j + 1].to_broadcast([P, P]), ident, t_p)
            stat_free[n] = [t, t_p]
        else:
            wide = row[:, :].rearrange("p (j n) -> p j n", n=P // g)
            t_w = copy_act(wide, dst.unsqueeze(2).to_broadcast([P, nt * g, P // g]), t_p, row_free)
            stat_free[n] = [t_w, t_p]
            yield
            yield
            for j in range(nt):
                t = mm(bank[:, j * P:j * P + P], row[:, j * P:j * P + P], ident, t_w)
        yield
        t_row = copy_act(row[:, 0:width], bank[:, 0:width], t, row_free)
        misc.give(bank, t_row)
        return t_row, t_p

    x_tok = [[] for _ in range(DC)]

    class Norm:

        def __init__(self, gain, Xh, Xl, free, also=None, eng="pool"):
            self.eng = eng
            self.parts = [(gain, Xh, Xl)] + ([also] if also else [])
            self.Xs = [[None] * DC for _ in self.parts]
            self.X, self.free, self.n, self.t, self.rows = self.Xs[0], free, 0, None, None

        def chunk(self, c):
            if self.free is None:
                self.free = [Q.last["pe"]]
            flow.start(self.go(c), lasting=True)

        def go(self, c):
            xc = x[:, c, :]
            t_x = list(x_tok[c])
            his_ = []
            for gain, Xh, Xl in self.parts:
                his_.append(copy_act(Xh[:, c, :], xc, t_x, self.free, scale=pc(gain, c)))
            yield
            for (gain, Xh, Xl), t_h, X in zip(self.parts, his_, self.Xs):
                t_l = stt(Xl[:, c, :], xc, pc(gain, c), Xh[:, c, :].bitcast(F), MUL, SUB, t_h, self.free)
                x_tok[c].append(t_l)
                X[c] = (Xh[:, c, :], Xl[:, c, :], t_l)
            if c == 0:
                self.t = func(ACT.Square, acc[:, :], xc, t_x, rs_state["acc"])
                x_tok[c].append(self.t)
            else:
                sq, fr = yield from take(sq_pool)
                t_s = func(ACT.Square, sq[:, :], xc, t_x, fr)
                x_tok[c].append(t_s)
                yield
                while self.n < c:
                    yield
                self.t = tt(acc[:, :], acc[:, :], sq[:, :], ADD, t_s, self.t, eng=self.eng)
                sq_pool.give(sq, self.t)
            self.n += 1

        def finish(self):
            flow.start(self.fin(), lasting=True)

        def fin(self):
            while self.n < DC:
                yield
            for _ in range(3):
                yield
            t_row, t_tok = yield from inv_rms(acc, self.t, 1.0 / D, rsrow, rs_state["row"],
                                              tok_out=(rstok[:, 0:NT], rs_state["tok"]))
            rs_state["acc"] = [t_row]
            rs_state["row"], rs_state["tok"] = [], [t_row]
            self.rows = (t_row, t_tok)

        def row(self):
            flow.need(lambda: self.rows)
            return self.rows[0]

        def tok(self):
            flow.need(lambda: self.rows)
            return self.rows[1]

    def leave_rows(*toks):
        rs_state["row"] = rs_state["row"] + flat(toks)

    def leave_tok(*toks):
        rs_state["tok"] = rs_state["tok"] + flat(toks)

    def evac(out, bank, t, norm, *w, scale=None):
        if scale is None:
            t1 = tt(out, bank[:, :], rsrow[:, :], MUL, t, norm.row(), w)
        else:
            t1 = stt(out, bank[:, :], scale, rsrow[:, :], MUL, MUL, t, norm.row(), w)
        main.give(bank, t1)
        leave_rows(t1)
        return t1

    def evac_steps(out, bank, t, norm, *w, scale=None):
        while norm.rows is None:
            yield
        return evac(out, bank, t, norm, *w, scale=scale)

    def add_to_x(c, bank, t):
        t1 = tt(x[:, c, :], bank[:, :], x[:, c, :], ADD, t, x_tok[c])
        main.give(bank, t1)
        x_tok[c] = [t1]

    def two_parts(src, h, lo, t, free):
        t_h = copy_act(h, src, t, free)
        yield
        t_l = tt(lo, src, h.bitcast(F), SUB, t_h, free)
        return t_l

    s_out = Slot(sem("s_out"))
    s_in = [Slot(sem(f"s_in{i}")) for i in range(3)]

    W.first(1)
    t_xin = [Q.dma("sp", lambda e, c=c: e.dma_start(x[:, c, :], dram["x"][c * P:c * P + P, :]),
                   Slot(sem(f"s_x{c}"))) for c in range(DC)]
    t_par = Q.dma("act", lambda e: e.dma_start(par[:, :], dram["par"]), s_in[1])
    t_keep = Q.dma("act", lambda e: e.dma_start(keep[:, :], dram["keep"]), s_in[0])
    early = ExitStack()
    once = sb(early, [P, N_ONCE], side="right")
    tabs = [sb(early, [8, n], side="right") for n in (L1, L2)]
    s_tab = [Slot(sem("s_tab0")), Slot(sem("s_tab1"))]
    t_mhalf = memset(mhalf[:, :], -0.5)
    t_id = copy_dve(identb[:, :], ident, t_keep)
    t_idr = copy_dve(identr[:, :], keep[0:32, 0:32], t_keep)
    t_mk = copy_dve(maskb[:, :], keep[:, 3 * P + 2:4 * P + 2], t_keep)
    h0 = PAR["scw"][0]
    t_half = ts(par[:, h0:h0 + 120], par[:, h0:h0 + 120], 0.5, None, MUL, None, t_par)

    t_once, t_tabs = [], []

    def load_once():
        t_once.append(Q.dma("act", lambda e: e.dma_start(once[:, :], dram["once"]), s_in[2]))

    def bias_tables():
        at = 0
        for name, key, ln, tab, slot in (("rel", "tab1", L1, tabs[0], s_tab[0]), ("rel2", "tab2", L2, tabs[1], s_tab[1])):
            oh, m = once[0:32, at:at + ln], once[0:8, at + ln:at + 2 * ln]
            at += 2 * ln
            for a in range(0, ln, 320):
                n = min(320, ln - a)
                bank, bf = yield from take(misc)
                t = mm(bank[0:8, 0:n], pc(name, 0, 8)[0:32, :], oh[:, a:a + n], bf, t_once, t_par)
                yield
                yield
                t = tt(tab[:, a:a + n], m[:, a:a + n], bank[0:8, 0:n], SUB, t)
                misc.give(bank, t)
            t_tabs.append(put_table(key, tab, ln, slot, t))
            yield

    def put_table(key, tab, ln, slot, t):
        return Q.dma("act", lambda e: e.dma_start(dram[key], tab[:, 0:ln].unsqueeze(1).to_broadcast([8, P, ln])), slot, t)

    A = ExitStack()
    XS = [sb(A, [P, 4, S]) for _ in range(2)]
    BC = [sb(A, [P, 2, S]) for _ in range(2)]
    Btok, cbm = sb(A, [P, NT, P]), sb(A, [P, NT, P])
    xdt, xds = sb(A, [P, NT, S]), sb(A, [P, 3, S])
    St = sb(A, [P, 3, S])
    ZT = [sb(A, [P, 4, S]) for _ in range(2)]
    hd = Pool([sb(A, [P, S]) for _ in range(4)])
    ep = Pool([sb(A, [P, S]) for _ in range(2)])
    us = [sb(A, [P, S + 4]) for _ in range(3)]
    rg = sb(A, [P, S])
    csh, csl = sb(A, [32, S], R), sb(A, [32, S], R)
    dts, asb, css, dst_, ctot = (sb(A, [P, NT * 32]) for _ in range(5))
    rg_tok = sb(A, [P, 4])

    t_pad = [memset(u[:, 0:4], 0.0) for u in us]
    u_pool = Pool(us, t_pad)

    n1 = Norm("ssm_ln", XAh, XAl, [t_par, t_half], eng="dve")
    for c in range(DC):
        x_tok[c] = [t_xin[c]]
        n1.chunk(c)
    W.prepare(0)
    flow.tick()
    flow.tick()
    n1.finish()
    X = n1.X

    dk = {}

    def by_block(ap, n=32):
        return ap.rearrange("p (j h) -> p j h", h=n)

    def decays(tmp, steps):
        t = yield from steps
        yield
        bank, t = yield from by_token(tmp, 32, t)
        t = tt(by_block(dts[:, :]), by_block(bank[:, 0:P]), pc("dtb", 0, 32).unsqueeze(1).to_broadcast([P, NT, 32]), ADD, t)
        misc.give(bank, t)
        hd.give(tmp, t)
        t = ts(asb[:, :], dts[:, :], -1.0, None, MUL, None, t)
        t = tt(asb[:, :], asb[:, :], dts[:, :], MIN, t)
        t_ea = func(ACT.Exp, ctot[:, 0:32], pc("alog", 0, 32))
        yield
        t = func(ACT.Exp, asb[:, :], asb[:, :], t)
        t = func(ACT.Ln, asb[:, :], asb[:, :], t, bias=1.0)
        yield
        dk["dt"] = t_dt = stt(dts[:, :], dts[:, :], 0.0, asb[:, :], MAX, ADD, t)
        for j in range(NT):
            b = slice(32 * j, 32 * j + 32)
            t_a = stt(asb[:, b], dts[:, b], -1.0, ctot[:, 0:32], MUL, MUL, t_dt, t_ea)
        bank, bf = yield from take(misc)
        yield
        yield
        yield
        mm(bank[:, 0:P], tri, asb[:, :], bf, t_a)
        t = mm(bank[:, P:2 * P], ones, asb[:, :])
        yield
        dk["cs"] = t_cs = copy_dve(css[:, :], bank[:, 0:P], t)
        t_sub = tt(dst_[:, :], bank[:, P:2 * P], css[:, :], SUB, t_cs)
        yield
        dk["ct"] = t_ct = func(ACT.Exp, ctot[:, :], bank[:, P:2 * P], t_sub, t_a)
        misc.give(bank, t_ct)
        dk["ds"] = func(ACT.Exp, dst_[:, :], dst_[:, :], t_sub)
        bank, bf = yield from take(misc)
        for j in range(NT):
            t = turn(bank[0:32, j * P:j * P + P], css[:, 32 * j:32 * j + 32], bf, t_cs)
        yield
        t = copy_act(csh[:, :], bank[0:32, :], t)
        yield
        dk["csT"] = t = tt(csl[:, :], bank[0:32, :], csh[:, :].bitcast(F), SUB, t)
        misc.give(bank, t)

    st = {"xs": [[], []], "bc": [[], []], "btok": [], "cbm": [], "xdt": [], "xds": [], "St": [], "zt": [[], []], "rg": []}
    got = {}
    ended = set()

    def conv_silu(bank, ft, dst, t, dst_free, key):
        ub, uf = yield from take(u_pool)
        t = yield from evac_steps(ub[:, 4:S + 4], bank, t, n1, uf)
        yield
        t = func(ACT.Identity, dst, ub[:, 1:S + 1], t, dst_free, bias=pc("scb", ft), scale=pc("scw", 4 * ft))
        yield
        for k in range(1, 4):
            t = stt(dst, ub[:, 1 + k:S + 1 + k], pc("scw", 4 * ft + k), dst, MUL, ADD, t)
        yield
        t_h = func(ACT.Tanh, ub[:, 4:S + 4], dst, t)
        yield
        t = stt(dst, ub[:, 4:S + 4], 1.0, dst, ADD, MUL, t_h)
        u_pool.give(ub, t)
        got[key] = t

    def group_in(g):
        b = g % 2
        flow.need(lambda: g < 2 or ("out", g - 2) in ended)
        for i in range(6):
            if g == 0 and i == 2:
                load_once()
                tmp, free = hd.take()
                flow.start(decays(tmp, thin("ssm_in", 5120, 32, n1, tmp, free)), now=True)
            ft = 16 + 4 * i + g if i < 2 else 4 * g + i - 2
            dst, free = (BC[b][:, i, :], st["bc"][b]) if i < 2 else (XS[b][:, i - 2, :], st["xs"][b])
            bank, bf = grab(main)
            t = proj(bank[:, :], "ssm_in", 2048 + ft * P, X, DC, bf)
            flow.start(conv_silu(bank, ft, dst, t, free, ("in", g, i)), now=True)

    def silu_z(z, t, key):
        ub, uf = yield from take(u_pool)
        t_h = func(ACT.Tanh, ub[:, 4:S + 4], z, t, uf)
        yield
        t = stt(z, ub[:, 4:S + 4], 1.0, z, ADD, MUL, t_h)
        u_pool.give(ub, t)
        got[key] = t

    def group_z(g):
        flow.need(lambda: g < 2 or ("gate", g - 2) in ended)
        free = list(st["zt"][g % 2])
        for i in range(4):
            z = ZT[g % 2][:, i, :]
            bank, bf = grab(main)
            t = proj(bank[:, :], "ssm_in", (4 * g + i) * P, X, DC, bf)
            t = evac(z, bank, t, n1, free, scale=0.5)
            flow.start(silu_z(z, t, ("z", g, i)))

    def heads(ap):
        return ap.rearrange("p (h d) -> p h d", h=8)

    def each_chunk(col):
        return col.unsqueeze(2).to_broadcast([P, 8, 64])

    def state(g):
        b = g % 2
        BT, CT = BC[b][:, 0, :], BC[b][:, 1, :]
        while not all(("in", g, i) in got for i in range(2)):
            yield
        tB, tC = got["in", g, 0], got["in", g, 1]
        yield
        yield
        bank, bf = yield from take(misc)
        for c in range(NT):
            t = turn(bank[:, c * P:c * P + P], BT[:, c * P:c * P + P], bf, tB)
        bank2, bf2 = yield from take(misc)
        for c in range(NT):
            a = slice(c * P, c * P + P)
            t2 = mm(bank2[:, a], BT[:, a], CT[:, a], bf2, tB, tC)
        yield
        t_bt = copy_act(Btok[:, :, :], bank[:, :].rearrange("p (c n) -> p c n", c=NT), t, st["btok"])
        misc.give(bank, t_bt)
        t_cb = tt(cbm[:, :, :], bank2[:, :].rearrange("p (c n) -> p c n", c=NT),
                  tri.unsqueeze(1).to_broadcast([P, NT, P]), MUL, t2, st["cbm"])
        misc.give(bank2, t_cb)
        while not (all(("in", g, i) in got for i in range(2, 6)) and "csT" in dk):
            yield
        yield
        yield
        t_xdt, t_xds, t_S = [], [], []
        for c in range(NT):
            bank, bf = yield from take(misc)
            for i in range(4):
                t = turn(bank[:, i * P:i * P + P], XS[b][:, i, c * P:c * P + P], bf, got["in", g, 2 + i])
            yield
            hs = slice(32 * c + 8 * g, 32 * c + 8 * g + 8)
            t = tt(heads(xdt[:, c, :]), heads(bank[:, :]), each_chunk(dts[:, hs]), MUL, t, dk["dt"], st["xdt"])
            misc.give(bank, t)
            t_xdt.append(t)
            if c < 3:
                t_xds.append(tt(heads(xds[:, c, :]), heads(xdt[:, c, :]), each_chunk(dst_[:, hs]), MUL, t, dk["ds"],
                                st["xds"], eng="pool"))
        for c in range(3):
            bank, bf = yield from take(misc)
            t = mm(bank[:, :], Btok[:, c, :], xds[:, c, :], bf, t_bt, t_xds[c])
            st["btok"] = st["xds"] = [t]
            if c > 0:
                hs = slice(32 * c + 8 * g, 32 * c + 8 * g + 8)
                t_m = tt(heads(St[:, c, :]), heads(St[:, c - 1, :]), each_chunk(ctot[:, hs]), MUL, t_S[-1], dk["ct"],
                         st["St"], eng="pool")
            yield
            if c == 0:
                t = copy_act(St[:, 0, :], bank[:, :], t, st["St"])
            else:
                t = tt(St[:, c, :], bank[:, :], St[:, c, :], ADD, t, t_m)
            misc.give(bank, t)
            t_S.append(t)
        return t_cb, t_xdt, t_S

    def pair_of_heads(g, pair, t_cb, t_xdt, t_S, uses):
        b = g % 2
        CT = BC[b][:, 1, :]
        h = 8 * g + 2 * pair
        bk = yield from take(misc, 2)
        ds = yield from take(hd, 2)
        for k, (bank, bf) in enumerate(bk):
            sel = identr[:, h + k:h + k + 1].to_broadcast([32, P])
            mm(bank[:, :], sel, csl[:, :], bf, dk["csT"], t_idr, stop=False)
            t = mm(bank[:, :], sel, csh[:, :], start=False)
        yield
        t_d = []
        for k, (bank, _) in enumerate(bk):
            d, df = ds[k]
            for c in range(NT):
                a = slice(c * P, c * P + P)
                col = 32 * c + h + k
                t_1 = ts(d[:, a], bank[:, a], css[:, col:col + 1], 0.0, SUB, MIN, t, dk["cs"], df)
            t_d.append(t_1)
        yield
        e_, ef = yield from take(ep)
        for k, (bank, _) in enumerate(bk):
            r = slice(64 * k, 64 * k + 64)
            t_e = func(ACT.Exp, e_[r, P:S], bank[r, P:S], t, t_d, ef)
            misc.give(bank, t_e)
        t_x = [exp_(d, t_1) for (d, _), t_1 in zip(ds, t_d)]
        yield
        t_g = [tt(d[:, :], d[:, :], cbm[:, :, :].rearrange("p c n -> p (c n)"), MUL, t, t_cb, eng="pool")
               for (d, _), t in zip(ds, t_x)]
        bo, bof = yield from take(misc)
        for c in range(1, NT):
            t_o = mm(bo[:, c * P:c * P + P], St[:, c - 1, pair * P:pair * P + P], CT[:, c * P:c * P + P], bof, t_S,
                     got["in", g, 1])
        yield
        t_2 = tt(e_[:, P:S], bo[:, P:S], e_[:, P:S], MUL, t_o, t_e)
        misc.give(bo, t_2)
        yield
        by, byf = yield from take(misc)
        yield
        for k, (d, _) in enumerate(ds):
            hl = 2 * pair + k
            for c in range(NT):
                t_m = mm(by[64 * k:64 * k + 64, c * P:c * P + P], xdt[:, c, 64 * hl:64 * hl + 64],
                         d[:, c * P:c * P + P], byf, t_g[k], t_xdt[c])
            hd.give(d, t_m)
        yield
        xs = XS[b][:, pair, :]
        t_1 = stt(xs, xs, pc("sd", 4 * g + pair), by[:, :], MUL, ADD, t_m, t_xdt, got["in", g, 2 + pair])
        misc.give(by, t_1)
        yield
        t_3 = tt(xs[:, P:S], xs[:, P:S], e_[:, P:S], ADD, t_1, t_2, eng="pool")
        ep.give(e_, t_3)
        got["y", g, pair] = [t_1, t_3]
        uses.append([t_m, t_o] + t_g)

    def exp_(d, t):
        return func(ACT.Exp, d[:, :], d[:, :], t)

    def ssd():
        for g in range(4):
            shared = yield from state(g)
            uses = []
            for pair in range(4):
                flow.start(pair_of_heads(g, pair, *shared, uses))
                yield
                yield
            while len(uses) < 4:
                yield
            st["cbm"] = st["xdt"] = st["St"] = st["bc"][g % 2] = flat(uses)
            flow.start(group_out(g))

    Y, y_parts, late = {}, [], ExitStack()

    def group_out(g):
        b = g % 2
        while not all(("z", g, i) in got and ("y", g, i) in got for i in range(4)):
            yield
        t_a, ty = None, []
        for i in range(4):
            xs = XS[b][:, i, :]
            t = tt(xs, xs, ZT[b][:, i, :], MUL, got["y", g, i], got["z", g, i])
            ty.append(t)
        st["zt"][b] = ty
        ended.add(("gate", g))
        while not (g == 0 or ("out", g - 1) in ended) or n1.rows is None:
            yield
        for i in range(4):
            xs = XS[b][:, i, :]
            if i == 0:
                t_a = func(ACT.Square, acc[:, :], xs, ty[i], rs_state["acc"])
            else:
                sq, fr = yield from take(sq_pool)
                t_s = func(ACT.Square, sq[:, :], xs, ty[i], fr)
                yield
                t_a = tt(acc[:, :], acc[:, :], sq[:, :], ADD, t_s, t_a, eng="pool")
                sq_pool.give(sq, t_a)
        for _ in range(7):
            yield
        t_r, _ = yield from inv_rms(acc, t_a, 1.0 / 512, rg, st["rg"])
        rs_state["acc"] = [t_r]
        yield
        if g == 0:
            while len(t_tabs) < 2:
                yield
            early.close()
            y_parts.extend(sb(late, [P, 4, S], R, side="right") for _ in range(2))
            free = [t_tabs, t_once]
        elif g < 3:
            while ("proj", g - 1) not in ended:
                yield
            free = [Q.last["pe"]]
        else:
            y_parts[:] = XAh, XAl
            free = [Q.last["pe"]]
        Y[g] = [None] * 4
        for i in range(4):
            xs = XS[b][:, i, :]
            h, lo = (part_[:, i, :] for part_ in y_parts)
            t = stt(xs, xs, pc("sng", 4 * g + i), rg[:, :], MUL, MUL, t_r, ty[i])
            st["rg"] = [t]
            yield
            t_l = yield from two_parts(xs, h, lo, t, free)
            Y[g][i] = (h, lo, t_l)
        st["xs"][b] = [y[2] for y in Y[g]]
        ended.add(("out", g))

    def out_proj(g, post=None):
        flow.need(lambda: g in Y)
        for pairt in range(4):
            bk = [grab(main), grab(main)]
            u, wh, wl, tw = W.unit("ssm_out", 4 * g, 4, 2 * pairt * P, 2 * P)
            for k in range(2):
                c_ = 2 * pairt + k
                for c in range(4):
                    if c % 2 == 0:
                        flow.tick()
                    yh, yl, ty = operand(Y[g], c)
                    a = slice(k * P, k * P + P)
                    mm(bk[k][0][:, :], wl[:, c, a], yh, tw, ty, bk[k][1], start=c == 0, stop=False)
                    mm(bk[k][0][:, :], wh[:, c, a], yl, start=False, stop=False)
                    t = mm(bk[k][0][:, :], wh[:, c, a], yh, start=False, stop=c == 3)
                add_to_x(c_, bk[k][0], t)
                if post:
                    post(c_)
            W.done(u, t)
        ended.add(("proj", g))

    flow.start(ssd())
    group_in(0)
    flow.start(bias_tables())
    group_in(1)
    group_z(0)
    group_z(1)
    group_in(2)
    out_proj(0)
    group_z(2)
    group_in(3)
    out_proj(1)
    group_z(3)
    out_proj(2)
    flow.settle()
    A.close()
    late.close()
    XBh, XBl = sb(ctx, [P, DC, S], R, side="right"), sb(ctx, [P, DC, S], R, side="right")
    nf = Norm("ffn_ln0", XBh, XBl, Q.ends())
    out_proj(3, nf.chunk)
    nf.finish()

    def ffn(up, gate_cols, up_name, up_cols, down, norm, conv, post):
        sc = ExitStack()
        before = Q.ends()
        X = norm.X
        Hh, Hl = sb(sc, [P, 12, S], R), sb(sc, [P, 12, S], R)
        v_pool = Pool([sb(sc, [P, S]) for _ in range(6)], before)
        u_pool = None
        if conv:
            us = [sb(sc, [P, S + 4]) for _ in range(3)]
            u_pool = Pool(us, [memset(u[:, 0:4], 0.0, before) for u in us], before)
        h_free = flat(before)
        H = [None] * 12

        def conv_steps(ub, v, vf, ft, t):
            cw, cb = conv
            t = func(ACT.Identity, v[:, :], ub[:, 2:S + 2], t, vf, bias=pc(cb, ft), scale=pc(cw, 3 * ft))
            yield
            for k in (1, 2):
                t = stt(v[:, :], ub[:, 2 + k:S + 2 + k], pc(cw, 3 * ft + k), v[:, :], MUL, ADD, t)
            u_pool.give(ub, t)
            return t

        def first_steps(bank, t, ft):
            v, vf = yield from take(v_pool)
            if conv is None:
                t = yield from evac_steps(v[:, :], bank, t, norm, vf)
                return v, t
            ub, uf = yield from take(u_pool)
            t = yield from evac_steps(ub[:, 4:S + 4], bank, t, norm, uf)
            yield
            t = yield from conv_steps(ub, v, vf, ft, t)
            return v, t

        def gate_steps(bank, t, ft, gate):
            v, t = yield from first_steps(bank, t, ft)
            yield
            gate.append((v, func(ACT.Silu, v[:, :], v[:, :], t)))

        def up_steps(bank, t, ft, gate, i, free):
            v, t = yield from first_steps(bank, t, ft)
            while not gate:
                yield
            v_gate, t_g = gate[0]
            t = tt(v[:, :], v[:, :], v_gate[:, :], MUL, t, t_g, eng="pool" if i != last_up else "dve")
            v_pool.give(v_gate, t)
            yield
            h, lo = Hh[:, i, :], Hl[:, i, :]
            t_l = yield from two_parts(v[:, :], h, lo, t, free)
            v_pool.give(v, t_l)
            H[i] = (h, lo, t_l)

        def tile(name, ft, col):
            bank, bf = grab(main)
            return bank, proj(bank[:, :], name, col + ft % FFC * P, X, DC, bf), ft

        for f0, nf_ in ((0, 12), (12, 10)):
            last_up = nf_ - 1
            for i in range(12):
                H[i] = None
            for f in range(f0, f0 + nf_):
                gate = []
                flow.start(gate_steps(*tile(up, f, gate_cols), gate), now=True)
                flow.start(up_steps(*tile(up_name, FFC + f, up_cols), gate, f - f0, h_free), now=True)
            for c in range(DC):
                bank, bf = grab(main)
                per = nf_ // 2
                for r in range(2):
                    u, wh, wl, tw = W.unit(down, f0 + r * per, per, c * P, P)
                    for k in range(per):
                        if k % 2 == 0:
                            flow.tick()
                        xh, xl, tx = operand(H, r * per + k)
                        i0 = r == 0 and k == 0
                        mm(bank[:, :], wl[:, k, :], xh, tw, tx, bf, start=i0, stop=False)
                        mm(bank[:, :], wh[:, k, :], xl, start=False, stop=False)
                        tok = mm(bank[:, :], wh[:, k, :], xh, start=False, stop=r == 1 and k == per - 1)
                    W.done(u, tok)
                add_to_x(c, bank, tok)
                if f0 and post:
                    post(c)
            h_free = [tok]
        flow.settle()
        sc.close()

    nq = Norm("attn_ln", XAh, XAl, None, also=("kv_ln", XBh, XBl))
    ffn("up0", 0, "up0", 2816, "down0", nf, ("fcw0", "fcb0"), nq.chunk)
    nq.finish()
    C = ExitStack()
    before = Q.ends()
    Qf, V = sb(C, [P, 8, S]), sb(C, [P, NT, D])
    kp = Pool([sb(C, [P, S]) for _ in range(3)], before)
    tbp = Pool([(sb(C, [P, S]), i) for i in range(2)], before)
    s_tb = [Slot(sem(f"s_tb{i}")) for i in range(2)]
    Lp = Pool([sb(C, [P, S]) for _ in range(10)], before)
    Op = Pool([sb(C, [P, S]) for _ in range(2)], before)
    sm = Pool([sb(C, [P, 8]) for _ in range(8)], before)
    lamt = sb(C, [P, 64])
    l4 = sb(C, [P, 8])
    rqp = Pool([sb(C, [P, S]) for _ in range(2)], before)
    qscale = sb(C, [P, 1])
    sbl = sb(C, [P, 1])

    t1 = tt(lamt[:, :], pc("lam", 0, 64), pc("lam", 64, 64), MUL, before)
    t1 = op("dve", lambda e: e.tensor_reduce(l4[:, 0:1], lamt[:, :], mybir.AxisListType.X, ADD), t1, before)
    t2 = tt(lamt[:, :], pc("lam", 128, 64), pc("lam", 192, 64), MUL, t1)
    t2 = op("dve", lambda e: e.tensor_reduce(l4[:, 1:2], lamt[:, :], mybir.AxisListType.X, ADD), t2)
    t3 = func(ACT.Exp, l4[:, 2:4], l4[:, 0:2], t2)
    t4 = tt(l4[:, 4:5], l4[:, 2:3], l4[:, 3:4], SUB, t3)
    t_lam = ts(l4[:, 5:6], l4[:, 4:5], LAM_INIT, None, ADD, None, t4)
    t_qs = ts(qscale[:, :], pc("qn"), -0.125, None, MUL, None, before)
    t_sb = ts(sbl[:, :], pc("subln"), 1.0 - LAM_INIT, None, MUL, None, before)

    kv = nq.Xs[1]
    tq, tk, tv, tb_of = {}, {}, {}, {}

    def head_norm(dst, bank, t, free, gain, t_gain, done, key):
        t1 = yield from evac_steps(dst, bank, t, nq, free)
        yield
        sq, fr = yield from take(sq_pool)
        t_s = func(ACT.Square, sq[:, :], dst, t1, fr)
        rq, rf = yield from take(rqp)
        yield
        yield
        t_r, _ = yield from inv_rms(sq, t_s, 1.0 / 64, rq, rf, groups=2)
        sq_pool.give(sq, t_r)
        yield
        t2 = stt(dst, dst, gain, rq[:, :], MUL, MUL, t_r, t_gain, t1)
        rqp.give(rq, t2)
        done[key] = t2

    def diff_q(h):
        bank, bf = grab(main)
        t = proj(bank[:, :], "q_w", h * P, nq.X, DC, bf)
        flow.start(head_norm(Qf[:, h, :], bank, t, before, qscale[:, :], t_qs, tq, h), now=True)

    k_of = {}

    def diff_k(h):
        bank, bf = grab(main)
        t = proj(bank[:, :], "kv_w", h * P, kv, DC, bf)
        k, kf = grab(kp)
        k_of[h] = k
        flow.start(head_norm(k[:, :], bank, t, kf, pc("kn"), None, tk, h), now=True)

    def diff_v(q):
        bk, outs = proj_tok("kv_w", D + 256 * q, 256, kv, DC, 4)
        nq.tok()
        toks = []
        for j, (out, t) in enumerate(outs):
            toks.append(copy_act(V[:, j, 256 * q:256 * q + 256], out, t, nq.rows[1], before, scale=rstok[:, j:j + 1]))
        for i, (bank, _) in enumerate(bk):
            main.give(bank, toks[2 * i + 1])
        leave_tok(toks)
        tv[q] = toks

    def skewed(tab, n, w):
        return tab.rearrange("p n -> (p n)")[127:127 + P * (n - 1)].rearrange("(p n) -> p n", n=n - 1)[:, 0:w]

    def get_tab1(tb, slot, h, free):
        return Q.dma("sp", lambda e: e.dma_start(tb[:, :], skewed(dram["tab1"][h], L1, S)), slot, free, t_tabs)

    def shared_bank(owner):
        if owner["o"] is None:
            owner["o"] = ()
            owner["o"] = yield from take(misc)
        while not owner["o"]:
            yield
        return owner["o"]

    def diff_block(h, i, head):
        k = k_of[h]
        tb, t_tb = head["tb"]
        n = (i + 1) * P
        bk = yield from take(misc, 2)
        t_m = []
        for c in range(2):
            r = slice(64 * c, 64 * c + 64)
            t_m.append(mm(bk[c][0][:, 0:n], Qf[r, h, i * P:i * P + P], k[r, 0:n], bk[c][1], tq[h], tk[h]))
        head["k"] += t_m
        yield
        Ls = yield from take(Lp, 2)
        s8, sf = yield from take(sm)
        for c in range(2):
            t_m[c] = add_min(Ls[c][0][:, 0:n], bk[c][0][:, 0:n], tb[:, (3 - i) * P:(3 - i) * P + n], s8[:, c:c + 1],
                             t_m[c], t_tb, Ls[c][1], sf)
            misc.give(bk[c][0], t_m[c])
        head["tbu"] += t_m
        yield
        (a, _), (b, _) = Ls
        t_e = [func(ACT.Exp, L[:, 0:n], L[:, 0:n], t, bias=s8[:, c:c + 1], scale=-1.0, accum=s8[:, 2 + c:3 + c])
               for c, (L, t) in enumerate(zip((a, b), t_m))]
        yield
        t = recip(s8[:, 4:6], s8[:, 2:4], t_e)
        t_l = tt(s8[:, 6:7], s8[:, 5:6], l4[:, 5:6], MUL, t, t_lam)
        t_p = ts(b[:, 0:n], b[:, 0:n], s8[:, 6:7], 1.0, MUL, MUL, t_l, eng="pool")
        yield
        t_a = stt(a[:, 0:n], a[:, 0:n], s8[:, 4:5], b[:, 0:n], MUL, SUB, t_p, t)
        Lp.give(b, t_a)
        sm.give(s8, t_a)
        yield
        yield
        bank, bf = yield from take(misc)
        for j in range(i + 1):
            t = turn(bank[:, j * P:j * P + P], a[:, j * P:j * P + P], t_a, bf)
        yield
        t = copy_act(a[:, 0:n], bank[:, 0:n], t)
        misc.give(bank, t)
        yield
        while h // 2 not in tv:
            yield
        ob, of = yield from shared_bank(head)
        for j in range(i + 1):
            t_o = mm(ob[:, i * P:i * P + P], V[:, j, h * P:h * P + P], a[:, j * P:j * P + P], of, t, tv[h // 2],
                     start=j == 0, stop=j == i)
        Lp.give(a, t_o)
        head["av"].append(t_o)

    o_out = [None] * DC

    def diff_head(h):
        head = {"k": [], "tbu": [], "av": [], "o": None}
        (tb, n), tbf = yield from take(tbp)
        head["tb"] = (tb, get_tab1(tb, s_tb[n], h, tbf))
        while not (h in tq and h in tk):
            yield
        for i in range(NT):
            flow.start(diff_block(h, i, head))
            yield
        flow.start(diff_end(h, head, (tb, n)))

    def diff_end(h, head, tb):
        while len(head["k"]) < 8:
            yield
        kp.give(k_of[h], head["k"])
        while len(head["tbu"]) < 8:
            yield
        tbp.give(tb, head["tbu"])
        while len(head["av"]) < NT:
            yield
        yield
        ob, of = yield from take(Op)
        bank = head["o"][0]
        t = copy_dve(ob[:, :], bank[:, :], head["av"], of)
        misc.give(bank, t)
        yield
        sq, fr = yield from take(sq_pool)
        t_s = func(ACT.Square, sq[:, :], ob[:, :], t, fr)
        rq, rf = yield from take(rqp)
        yield
        t_r, _ = yield from inv_rms(sq, t_s, 1.0 / P, rq, rf)
        sq_pool.give(sq, t_r)
        while "q" not in ended:
            yield
        t = stt(ob[:, :], ob[:, :], sbl[:, 0:1], rq[:, :], MUL, MUL, t_r, t_sb)
        rqp.give(rq, t)
        hh, ll = XAh[:, h, :], XAl[:, h, :]
        yield
        t_l = yield from two_parts(ob[:, :], hh, ll, t, t_q_end)
        Op.give(ob, t_l)
        o_out[h] = (hh, ll, t_l)

    def in_turn(gens):
        for gen in gens:
            yield from gen

    def out_part(name, r0, n, Os, post=None):
        for pairt in range(4):
            bk = [grab(main), grab(main)]
            u, wh, wl, tw = W.unit(name, r0, n, 2 * pairt * P, 2 * P)
            for k in range(2):
                for c in range(n):
                    if c % 2 == 0:
                        flow.tick()
                    oh, ol, to = operand(Os, r0 + c)
                    a = slice(k * P, k * P + P)
                    mm(bk[k][0][:, :], wl[:, c, a], oh, tw, to, bk[k][1], start=c == 0, stop=False)
                    mm(bk[k][0][:, :], wh[:, c, a], ol, start=False, stop=False)
                    t = mm(bk[k][0][:, :], wh[:, c, a], oh, start=False, stop=c == n - 1)
                add_to_x(2 * pairt + k, bk[k][0], t)
                if post:
                    post(2 * pairt + k)
            W.done(u, t)

    flow.start(in_turn([diff_head(h) for h in range(8)]))
    diff_k(0)
    diff_q(0)
    diff_v(0)
    diff_k(1)
    for h in range(1, 8):
        diff_q(h)
    t_q_end = Q.last["pe"]
    ended.add("q")
    for h in range(2, 8):
        diff_k(h)
        if h in (2, 3, 4):
            diff_v(h - 1)
    out_part("attn_out", 0, 4, o_out)
    n_f1 = Norm("ffn_ln1", XBh, XBl, None)
    out_part("attn_out", 4, 4, o_out, n_f1.chunk)
    n_f1.finish()
    flow.settle()
    C.close()
    nm = Norm("mix", XAh, XAl, None)
    ffn("up1", 0, "up1", 2816, "down1", n_f1, ("fcw1", "fcb1"), nm.chunk)
    nm.finish()

    G = ExitStack()
    before = Q.ends()
    X = nm.X
    s_sp = Slot(sem("s_spill"))
    flow.need(lambda: nm.n == DC)
    t_spill = Q.dma("act", lambda e: e.dma_start(dram["spill"].rearrange("(c p) n -> p c n", p=P), x[:, :, :]), s_sp, x_tok)
    part = x
    Qb, Kb, Vb = sb(G, [P, 4, S]), sb(G, [P, 4, S]), sb(G, [P, NT, 512])
    MGh, MGl = sb(G, [P, 4, S], R), sb(G, [P, 4, S], R)
    us = [sb(G, [P, S + 4]) for _ in range(2)]
    u_pool = Pool(us, [memset(u[:, 0:4], 0.0, before) for u in us], before)
    vp = Pool([sb(G, [P, S]) for _ in range(4)], before)
    Lp = Pool([sb(G, [P, S]) for _ in range(5)], before)
    ckp = Pool([sb(G, [P, S]) for _ in range(2)], before)
    ckip = Pool([sb(G, [P, S]) for _ in range(2)], before)
    sm = Pool([sb(G, [P, 8]) for _ in range(8)], before)
    cfs, nc_ = sb(G, [P, 32]), sb(G, [P, 32])
    cTh, cTl = sb(G, [8, S], R), sb(G, [8, S], R)
    nsink = sb(G, [P, 8])
    rt = sb(G, [P, 4])
    tb2 = Pool([(sb(G, [P, 256]), i) for i in range(2)], before)
    s_tb2 = [Slot(sem(f"s_tb2{i}")) for i in range(2)]
    t_ns = ts(nsink[:, :], pc("sink", 0, 8), -1.0, None, MUL, None, before)
    xb_free = flat([before])
    fg = {}

    def forget(tmp, steps):
        t = yield from steps
        yield
        bank, t = yield from by_token(tmp, 8, t)
        t = tt(by_block(cfs[:, :], 8), by_block(bank[:, 0:32], 8), pc("fbias", 0, 8).unsqueeze(1).to_broadcast([P, NT, 8]),
               ADD, t, before)
        misc.give(bank, t)
        ckp.give(tmp, t)
        t = ts(nc_[:, :], cfs[:, :], -1.0, None, MUL, None, t, before)
        t = tt(nc_[:, :], nc_[:, :], cfs[:, :], MIN, t)
        yield
        t = func(ACT.Exp, nc_[:, :], nc_[:, :], t)
        t = func(ACT.Ln, nc_[:, :], nc_[:, :], t, bias=1.0)
        yield
        t_lf = stt(cfs[:, :], cfs[:, :], 0.0, nc_[:, :], MIN, SUB, t)
        bank, bf = yield from take(misc)
        yield
        for j in range(NT):
            for i in range(j + 1):
                t = mm(bank[:, 8 * j:8 * j + 8], tri if i == j else ones, cfs[:, 8 * i:8 * i + 8], t_lf, bf,
                       start=i == 0, stop=i == j)
        yield
        t_c = copy_dve(cfs[:, :], bank[:, 0:32], t)
        fg["nc"] = ts(nc_[:, :], cfs[:, :], -1.0, None, MUL, None, t_c, t_lf)
        misc.give(bank, t_c)
        bank, bf = yield from take(misc)
        yield
        for j in range(NT):
            t = turn(bank[0:8, j * P:j * P + P], cfs[:, 8 * j:8 * j + 8], bf, t_c)
        yield
        t = copy_act(cTh[:, :], bank[0:8, :], t, before)
        yield
        fg["cT"] = t = tt(cTl[:, :], bank[0:8, :], cTh[:, :].bitcast(F), SUB, t, before)
        misc.give(bank, t)

    def scaled(name_col, dst, free, scale=None):
        bank, bf = grab(main)
        t = proj(bank[:, :], "w_in", name_col, X, DC, bf)
        return evac(dst, bank, t, nm, free, scale=scale)

    Ys = {0: [None] * 4, 1: [None] * 4, 2: [None] * 4}

    def conv_tile(i):
        v, vf = grab(vp)
        t_c = scaled(512 + i * P, v[:, :], vf)
        zb, zf = grab(u_pool)
        t_u = scaled(1024 + i * P, zb[:, 4:S + 4], zf)
        b = []
        flow.start(conv_steps(i, zb, v, t_c, t_u, b))
        w, wf = grab(vp)
        b.append((w, scaled(i * P, w[:, :], wf)))

    def conv_steps(i, zb, v, t_c, t_u, b):
        t1 = tt(zb[:, 4:S + 4], zb[:, 4:S + 4], v[:, :], MUL, t_u, t_c)
        yield
        t = copy_act(v[:, :], zb[:, 2:S + 2], t1, scale=pc("cw2", 3 * i))
        yield
        for k in (1, 2):
            t = stt(v[:, :], zb[:, 2 + k:S + 2 + k], pc("cw2", 3 * i + k), v[:, :], MUL, ADD, t)
        u_pool.give(zb, t)
        while not b:
            yield
        w, t_b = b[0]
        t = tt(w[:, :], w[:, :], v[:, :], MUL, t, t_b)
        vp.give(v, t)
        yield
        h, lo = XBh[:, 4 + i, :], XBl[:, 4 + i, :]
        t_l = yield from two_parts(w[:, :], h, lo, t, xb_free)
        vp.give(w, t_l)
        Ys[0][i] = (h, lo, t_l)

    t_part = [[t_spill] for _ in range(DC)]
    mg = [None] * DC

    def gate_steps(v, t, out):
        out.append(func(ACT.Tanh, v[:, :], v[:, :], t, scale=0.5))
        yield

    def sum_steps(i, c, v, t, last, free):
        yield
        if i == 0:
            t_part[c] = [t]
        elif not last:
            t_part[c] = [tt(part[:, c, :], part[:, c, :], v[:, :], ADD, t, t_part[c], eng="pool")]
            vp.give(v, t_part[c])
        else:
            t = tt(v[:, :], part[:, c, :], v[:, :], ADD, t, t_part[c])
            t_part[c] = [t]
            yield
            h, lo = (XBh[:, c, :], XBl[:, c, :]) if c < 4 else (MGh[:, c - 4, :], MGl[:, c - 4, :])
            t_h = copy_act(h, v[:, :], t, free, scale=0.5)
            yield
            t_l = stt(lo, v[:, :], 0.5, h.bitcast(F), MUL, SUB, t_h, free)
            vp.give(v, t_l)
            mg[c] = (h, lo, t_l)

    def branch_tile(i, c, last=False, free=None):
        v, vf = grab(vp)
        t = scaled(3848 + i * D + c * P, v[:, :], vf)
        gate = []
        flow.start(gate_steps(v, t, gate))
        bank, bf = grab(main)
        t = proj(bank[:, :], f"branch{i}", c * P, Ys[i], 4, bf, per=4)
        flow.need(lambda: gate)
        if i == 0:
            t = stt(part[:, c, :], v[:, :], 1.0, bank[:, :], ADD, MUL, t, gate, t_part[c])
            vp.give(v, t)
        else:
            t = stt(v[:, :], v[:, :], 1.0, bank[:, :], ADD, MUL, t, gate)
        main.give(bank, t)
        flow.start(sum_steps(i, c, v, t, last, free))

    def soft_steps(L, s8, n, t_den):
        t = recip(s8[:, 5:6], s8[:, 4:5], t_den)
        t_a = ts(L[:, 0:n], L[:, 0:n], s8[:, 5:6], None, MUL, None, t)
        sm.give(s8, t_a)
        for _ in range(3):
            yield
        bank, bf = yield from take(misc)
        for j in range(n // P):
            t = turn(bank[:, j * P:j * P + P], L[:, j * P:j * P + P], t_a, bf)
        yield
        t = copy_act(L[:, 0:n], bank[:, 0:n], t)
        misc.give(bank, t)
        yield
        return t

    def fin_pair(tile_, ch, Yd, i, free):
        while len(tile_["av"]) < 2 * NT:
            yield
        yield
        bank = tile_["o"][0]
        h, lo = XBh[:, ch, :], XBl[:, ch, :]
        t_l = yield from two_parts(bank[:, :], h, lo, tile_["av"], free)
        misc.give(bank, t_l)
        Yd[i] = (h, lo, t_l)

    def get_tab2(tb, slot, h, free):
        return Q.dma("sp", lambda e: e.dma_start(tb[:, :], skewed(dram["tab2"][h], L2, 256)), slot, free, t_tabs)

    sq_, sk_, sv_ = {}, [], []

    def swa_block(tile, half, i, tile_, tb, t_tb, tbu):
        h = tile + 4 * half
        r = slice(64 * half, 64 * half + 64)
        a0 = max(i - 1, 0) * P
        n = (i + 1) * P - a0
        bank, bf = yield from take(misc)
        t = mm(bank[:, 0:n], Qb[r, tile, i * P:i * P + P], Kb[r, 0, a0:a0 + n], bf, sq_[tile], sk_)
        L, lf = yield from take(Lp)
        s8, sf = yield from take(sm)
        yield
        t = add_min(L[:, 0:n], bank[:, 0:n], tb[:, 256 - n:256], s8[:, 0:1], t, t_tb, lf, sf)
        misc.give(bank, t)
        tbu.append(t)
        t = tt(s8[:, 1:2], s8[:, 0:1], nsink[:, h:h + 1], MIN, t, t_ns)
        yield
        t_e = func(ACT.Exp, L[:, 0:n], L[:, 0:n], t, bias=s8[:, 1:2], scale=-1.0, accum=s8[:, 2:3])
        t_s = func(ACT.Exp, s8[:, 3:4], s8[:, 1:2], t, bias=pc("sink", h), scale=1.0)
        yield
        t = tt(s8[:, 4:5], s8[:, 2:3], s8[:, 3:4], ADD, t_e, t_s)
        t = yield from soft_steps(L, s8, n, t)
        ob, of = yield from shared_bank(tile_)
        js = [i] if i == 0 else [i - 1, i]
        for m_, j in enumerate(js):
            t_o = mm(ob[r, i * P:i * P + P], Vb[:, j, r], L[:, m_ * P:m_ * P + P], of, t, sv_,
                     start=m_ == 0, stop=m_ == len(js) - 1)
        Lp.give(L, t_o)
        tile_["av"].append(t_o)

    def swa():
        for tile in range(4):
            tile_ = {"o": None, "av": []}
            while not (tile in sq_ and sk_):
                yield
            for half in range(2):
                (tb, n), tbf = yield from take(tb2)
                t_tb = get_tab2(tb, s_tb2[n], tile + 4 * half, tbf)
                tbu = []
                for i in range(NT):
                    flow.start(swa_block(tile, half, i, tile_, tb, t_tb, tbu))
                    yield
                    yield
                while len(tbu) < NT:
                    yield
                tb2.give((tb, n), tbu)
            flow.start(fin_pair(tile_, tile, Ys[2], tile, xb_free))
        ended.add("swa")

    fq_, fk_, fv_ = {}, {}, {}

    def fox_block(h, i, ck, t_ck, tile_, uses):
        tile, half = h // 2, h % 2
        r = slice(64 * half, 64 * half + 64)
        n = (i + 1) * P
        cki, cf = yield from take(ckip)
        t_ci = ts(cki[:, 0:n], ck[:, 0:n], nc_[:, 8 * i + h:8 * i + h + 1], 1.0, ADD, MUL, t_ck, fg["nc"], cf, eng="pool")
        uses.append(t_ci)
        bank, bf = yield from take(misc)
        mm(bank[:, 0:n], Qb[r, tile, i * P:i * P + P], Kb[r, tile, 0:n], bf, fq_[tile], fk_[tile], stop=False)
        t = mm(bank[:, i * P:n], identb[:, :], maskb[:, :], start=False)
        L, lf = yield from take(Lp)
        s8, sf = yield from take(sm)
        yield
        t = add_min(L[:, 0:n], bank[:, 0:n], cki[:, 0:n], s8[:, 0:1], t, t_ci, lf, sf)
        misc.give(bank, t)
        ckip.give(cki, t)
        yield
        t = func(ACT.Exp, L[:, 0:n], L[:, 0:n], t, bias=s8[:, 0:1], scale=-1.0, accum=s8[:, 4:5])
        yield
        t = yield from soft_steps(L, s8, n, t)
        ob, of = yield from shared_bank(tile_)
        for j in range(i + 1):
            t_o = mm(ob[r, i * P:i * P + P], Vb[:, j, 64 * h:64 * h + 64], L[:, j * P:j * P + P], of, t, fv_[h // 4],
                     start=j == 0, stop=j == i)
        Lp.give(L, t_o)
        tile_["av"].append(t_o)

    def fox():
        for tile in range(4):
            tile_ = {"o": None, "av": []}
            for half in range(2):
                h = 2 * tile + half
                while not (tile in fq_ and tile in fk_ and h // 4 in fv_ and "cT" in fg):
                    yield
                bank, bf = yield from take(misc)
                sel = identr[0:8, h:h + 1].to_broadcast([8, P])
                mm(bank[:, :], sel, cTl[:, :], bf, fg["cT"], t_idr, stop=False)
                t = mm(bank[:, :], sel, cTh[:, :], start=False)
                ck, ckf = yield from take(ckp)
                yield
                t_ck = copy_act(ck[:, :], bank[:, :], t, ckf)
                misc.give(bank, t_ck)
                uses = []
                for i in range(NT):
                    flow.start(fox_block(h, i, ck, t_ck, tile_, uses))
                    yield
                while len(uses) < NT:
                    yield
                ckp.give(ck, uses)
            flow.start(fin_pair(tile_, 4 + tile, Ys[1], tile, yf_free))

    tmp, free = ckp.take()
    flow.start(forget(tmp, thin("w_in", 3072, 8, nm, tmp, free)), now=True)

    def later(put, name_col, dst, scale=None):
        bank, bf = grab(main)
        t = proj(bank[:, :], "w_in", name_col, X, DC, bf)
        flow.start(later_steps(put, dst, bank, t, scale), now=True)

    def later_steps(put, dst, bank, t, scale):
        t = yield from evac_steps(dst, bank, t, nm, before, scale=scale)
        put(t)

    later(sk_.append, 3080 + 512, Kb[:, 0, :])
    later(lambda t: sq_.__setitem__(0, t), ("swaq", 0), Qb[:, 0, :], -0.125)
    t_rt = copy_dve(rt[:, :], rstok[:, 0:4], nm.tok(), before)
    leave_tok(t_rt)
    bk, outs = proj_tok("w_in", 3080 + 640, P, X, DC, 8)
    for j, (out, t) in enumerate(outs):
        t = copy_act(Vb[:, j, 0:P], out, t, t_rt, before, scale=rt[:, j:j + 1])
        sv_.append(t)
    main.give(bk[0][0], t)
    flow.start(swa())
    for i in range(1, 4):
        sq_[i] = scaled(("swaq", i), Qb[:, i, :], before, -0.125)
    for i in range(4):
        conv_tile(i)
    for c in range(DC):
        branch_tile(0, c)
    flow.need(lambda: "swa" in ended and all(Ys[2]))
    free_q = Q.ends()
    yf_free = [Q.last["pe"], before]
    flow.start(fox())
    for i in range(2):
        if i == 0:
            fk_[0] = scaled(2048, Kb[:, 0, :], free_q)
            fq_[0] = scaled(1536, Qb[:, 0, :], free_q, -0.125)
        bk, outs = proj_tok("w_in", 2560 + 256 * i, 256, X, DC, 4)
        toks = []
        for j, (out, t) in enumerate(outs):
            toks.append(copy_act(Vb[:, j, 256 * i:256 * i + 256], out, t, t_rt, free_q, scale=rt[:, j:j + 1]))
        for j, (bank, _) in enumerate(bk):
            main.give(bank, toks[2 * j + 1])
        fv_[i] = toks
        for j in (1,) if i == 0 else (2, 3):
            fk_[j] = scaled(2048 + j * P, Kb[:, j, :], free_q)
            fq_[j] = scaled(1536 + j * P, Qb[:, j, :], free_q, -0.125)
    for c in range(DC):
        branch_tile(2, c)
    flow.need(lambda: all(Ys[1]))
    mg_free = [Q.last["pe"], before]
    for c in range(DC):
        branch_tile(1, c, last=True, free=mg_free)
    flow.need(lambda: all(mg))
    s_re = Slot(sem("s_reload"))
    t_re = Q.dma("act", lambda e: e.dma_start(x[:, :, :], dram["spill"].rearrange("(c p) n -> p c n", p=P)), s_re,
                 t_part, t_spill)
    for c in range(DC):
        x_tok[c] = [t_re]
    nx = Norm("xattn", XAh, XAl, [Q.last["pe"]])
    for c in range(DC):
        bank, bf = grab(main)
        t = proj(bank[:, :], "mix_out", c * P, mg, DC, bf)
        add_to_x(c, bank, t)
        nx.chunk(c)
    nx.finish()
    flow.settle()
    G.close()
    mix_end = Q.ends()

    G = ExitStack()
    before = mix_end
    M = 256
    mem = sb(G, [P, DC, M])
    mh, ml = sb(G, [P, DC, M], R), sb(G, [P, DC, M], R)
    macc, msq = sb(G, [P, M]), sb(G, [P, M])
    mrow = sb(G, [P, M])
    mtok = sb(G, [P, 4])
    Kx, Vx = sb(G, [P, DC, M]), sb(G, [P, 2, D])
    qp = Pool([sb(G, [P, 2, S]) for _ in range(2)], before)
    Lp = Pool([sb(G, [P, M]) for _ in range(8)], before)
    ATp = Pool([sb(G, [P, 2, S]) for _ in range(2)], before)
    sm = Pool([sb(G, [P, 8]) for _ in range(8)], before)
    s_mem = Slot(sem("s_mem"))
    t_mem = Q.dma("act", lambda e: e.dma_start(mem[:, :, :], dram["mem"].rearrange("(c p) n -> p c n", p=P)), s_mem, before)
    MX = [None] * DC
    mrows = []

    def mem_norm():
        t_a = None
        for c in range(DC):
            g = pc("mem", c)
            t_h = copy_act(mh[:, c, :], mem[:, c, :], t_mem, before, scale=g)
            if c == 0:
                t_a = func(ACT.Square, macc[:, :], mem[:, c, :], t_mem, before)
            else:
                t_s = func(ACT.Square, msq[:, :], mem[:, c, :], t_mem, before, t_a)
                t_a = tt(macc[:, :], macc[:, :], msq[:, :], ADD, t_s, t_a, eng="pool")
            yield
            t_l = stt(ml[:, c, :], mem[:, c, :], g, mh[:, c, :].bitcast(F), MUL, SUB, t_h, before)
            MX[c] = (mh[:, c, :], ml[:, c, :], t_l)
        for _ in range(4):
            yield
        t = yield from inv_rms(macc, t_a, 1.0 / D, mrow, before, width=M, tok_out=(mtok[:, 0:2], before))
        mrows.extend(t)

    flow.start(mem_norm())
    xq_, OX = {}, [None] * DC
    t_kx, t_vx = {}, {}

    def xq(h):
        qb, qf = grab(qp)
        toks = []
        for i in range(2):
            bank, bf = grab(main)
            t = proj(bank[:, :], "xq", (2 * h + i) * P, nx.X, DC, bf)
            flow.start(xq_steps(h, qb, qf, i, bank, t, toks), now=True)

    def xq_steps(h, qb, qf, i, bank, t, toks):
        t = yield from evac_steps(qb[:, i, :], bank, t, nx, qf, scale=-1.0 / 16)
        toks.append(t)
        if i == 1:
            xq_[h] = (qb, toks)

    def xk(c):
        bank, bf = grab(main)
        t = proj(bank[:, 0:M], "xkv", c * P, MX, DC, bf)
        flow.need(lambda: mrows)
        t = tt(Kx[:, c, :], bank[:, 0:M], mrow[:, :], MUL, t, mrows[0], before)
        main.give(bank, t)
        t_kx[c] = t

    def xv(q):
        bk, outs = proj_tok("xkv", D + 256 * q, 256, MX, DC, 4, nt=2)
        flow.need(lambda: mrows)
        toks = [copy_act(Vx[:, j, 256 * q:256 * q + 256], out, t, mrows[1], before, scale=mtok[:, j:j + 1])
                for j, (out, t) in enumerate(outs)]
        main.give(bk[0][0], toks)
        t_vx[q] = toks

    def x_block(h, i, AT, atf, t_at, uses):
        qb, tq_ = xq_[h]
        bank, bf = yield from take(misc)
        for d in range(2):
            t = mm(bank[:, 0:M], qb[:, d, i * P:i * P + P], Kx[:, 2 * h + d, :], bf, tq_, t_kx[2 * h], t_kx[2 * h + 1],
                   start=d == 0, stop=d == 1)
        uses.append(t)
        L, lf = yield from take(Lp)
        s8, sf = yield from take(sm)
        yield
        t = row_min(s8[:, 0:1], bank[:, 0:M], t, sf)
        yield
        t = func(ACT.Exp, L[:, 0:M], bank[:, 0:M], t, lf, bias=s8[:, 0:1], scale=-1.0, accum=s8[:, 4:5])
        misc.give(bank, t)
        yield
        t = recip(s8[:, 5:6], s8[:, 4:5], t)
        t_a = ts(L[:, :], L[:, :], s8[:, 5:6], None, MUL, None, t)
        sm.give(s8, t_a)
        for _ in range(3):
            yield
        bank, bf = yield from take(misc)
        for j in range(2):
            t = turn(bank[:, j * P:j * P + P], L[:, j * P:j * P + P], t_a, bf)
        Lp.give(L, t)
        yield
        t = copy_act(AT[:, :, i * P:i * P + P], bank[:, 0:M].rearrange("p (j q) -> p j q", j=2), t, atf)
        misc.give(bank, t)
        t_at.append(t)

    def row_min(out, in_, *w):
        return op("dve", lambda e: e.tensor_reduce(out, in_, mybir.AxisListType.X, MIN), *w)

    def x_head(h):
        while not (h in xq_ and 2 * h + 1 in t_kx and h in t_vx):
            yield
        AT, atf = yield from take(ATp)
        t_at, uses = [], []
        for i in range(NT):
            flow.start(x_block(h, i, AT, atf, t_at, uses))
            yield
            yield
        flow.start(x_end(h, AT, t_at, uses))

    def x_end(h, AT, t_at, uses):
        while len(uses) < NT:
            yield
        qp.give(xq_[h][0], uses)
        while len(t_at) < NT:
            yield
        yield
        for d in range(2):
            bank, bf = yield from take(misc)
            for j in range(2):
                t = mm(bank[:, :], Vx[:, j, h * 256 + d * P:h * 256 + d * P + P], AT[:, j, :], bf, t_at, t_vx[h],
                       start=j == 0, stop=j == 1)
            if d == 1:
                ATp.give(AT, t)
            yield
            ch = 2 * h + d
            hh, ll = XBh[:, ch, :], XBl[:, ch, :]
            t_l = yield from two_parts(bank[:, :], hh, ll, t, mix_end)
            misc.give(bank, t_l)
            OX[ch] = (hh, ll, t_l)

    flow.start(in_turn([x_head(h) for h in range(4)]))
    xq(0)
    xq(1)
    for h in range(4):
        if h > 1:
            xq(h)
        xk(2 * h)
        xk(2 * h + 1)
        xv(h)
    out_part("xo", 0, 4, OX)
    n2 = Norm("ffn2", XAh, XAl, None)
    out_part("xo", 4, 4, OX, n2.chunk)
    n2.finish()
    flow.settle()
    G.close()

    fin_ = {"t": None, "n": 0, "x": {}}
    end_free = []

    def last(c):
        if not end_free:
            end_free.append(Q.last["pe"])
        flow.start(last_steps(c), lasting=True)

    def last_steps(c):
        xc, out = x[:, c, :], XBh[:, c, :].bitcast(F)
        t_x = x_tok[c]
        if c == 0:
            fin_["t"] = func(ACT.Square, acc[:, :], xc, t_x, rs_state["acc"])
        else:
            sq, fr = yield from take(sq_pool)
            t_s = func(ACT.Square, sq[:, :], xc, t_x, fr)
            yield
            fin_["t"] = tt(acc[:, :], acc[:, :], sq[:, :], ADD, t_s, fin_["t"], eng="dve" if c == DC - 1 else "pool")
            sq_pool.give(sq, fin_["t"])
        fin_["x"][c] = copy_act(xc, xc, t_x, fin_["t"], scale=pc("final", c))
        fin_["n"] += 1

    ffn("gate2", 0, "up2", 0, "down2", n2, None, last)

    def finish():
        t_r, _ = yield from inv_rms(acc, fin_["t"], 1.0 / D, rsrow, rs_state["row"])
        for c in range(DC):
            eng = "pool" if c in (1, 4, 7) else "dve"
            t = tt(x[:, c, :], x[:, c, :], rsrow[:, :], MUL, t_r, fin_["x"][c], eng=eng)
            send(c, t)

    def send(c, t):
        Q.dma("sp" if c % 2 else "act", lambda e: e.dma_start(dram["out"][c * P:c * P + P, :], x[:, c, :]), s_out, t)

    flow.need(lambda: fin_["n"] == DC)
    flow.start(finish())
    flow.need(lambda: not flow.live)
    return Q, W, sems, s_out


def weight_table(a):
    t = {
        "ssm_in": a["ssm_in_w"][0], "ssm_out": a["ssm_out_w"][0], "kv_w": a["kv_w"], "q_w": a["q_w"][0],
        "attn_out": a["attn_out_w"][0], "up0": a["ffn_up_w"][0], "up1": a["ffn_up_w"][1],
        "down0": a["ffn_down_w"][0], "down1": a["ffn_down_w"][1], "w_in": a["w_in_2"][0],
        "mix_out": a["w_mix_out_2"][0], "xq": a["w_xq_2"][0], "xkv": a["w_xkv_2"][0], "xo": a["w_xo_2"][0],
        "gate2": a["w_ffn_gate_2"][0], "up2": a["w_ffn_up_2"][0], "down2": a["w_ffn_down_2"][0],
        "branch0": a["w_branch_2"][0, 0], "branch1": a["w_branch_2"][0, 1], "branch2": a["w_branch_2"][0, 2],
    }
    t = {k: np.asarray(v) for k, v in t.items()}
    t["branch2"] = t["branch2"].reshape(2, 4, 64, D).transpose(1, 0, 2, 3).reshape(512, D)
    return t


def pack(plan, table):
    out = np.empty(plan[-1][-2] + P * plan[-1][-1], np.float32)
    for name, r0, nk, c0, ncol, off, n in plan:
        rows = table[name][r0 * P:(r0 + nk) * P]
        if isinstance(c0, tuple):
            c = 3080 + np.concatenate([np.arange(64) + 64 * c0[1], np.arange(64) + 64 * (c0[1] + 4)])
            b = rows[:, c]
        else:
            b = rows[:, c0:c0 + ncol]
        out[off:off + P * n] = b.reshape(nk, P, ncol).transpose(1, 0, 2).reshape(-1)
    return out


def build(nc, scratch, mk):
    with ExitStack() as ctx:
        _, W, _, _ = emit(scratch, ctx, None, {})
    plan, off = [], 0
    for w in W.want:
        n = w[2] * w[4]
        plan.append((*w, off, n))
        off += P * n
    dram = mk(off)
    with ExitStack() as ctx:
        Q, _, sems, s_out = emit(nc, ctx, plan, dram)
        Q.number(sems)
        block = ctx.enter_context(nc.Block())

        @block.tensor
        def _(e):
            Q.play("pe", e)

        @block.scalar
        def _(e):
            Q.play("act", e)

        @block.vector
        def _(e):
            Q.play("dve", e)

        @block.gpsimd
        def _(e):
            Q.play("pool", e)

        @block.sync
        def _(e):
            Q.play("sp", e)
            e.wait_ge(s_out.sem, 16 * s_out.n)

    return plan


def kernel(**inputs):
    import concourse.bacc as _bacc
    from concourse.bass_utils import run_bass_kernel_spmd as _run

    a = {k: np.asarray(v) for k, v in inputs.items()}
    nc = _bacc.Bacc("TRN2", target_bir_lowering=False, num_devices=1)
    scratch = _bacc.Bacc("TRN2", target_bir_lowering=False, num_devices=1)
    keep, once = constants()
    arrays = {
        "x": np.ascontiguousarray(a["x"][0].T), "mem": np.ascontiguousarray(a["mem_2"][0].T),
        "par": parameters(a), "keep": keep, "once": once,
    }

    def mk(n):
        dram = {k: nc.dram_tensor(f"in_{k}", v.shape, F, kind="ExternalInput").ap() for k, v in arrays.items()}
        dram["w"] = nc.dram_tensor("in_w", (n,), F, kind="ExternalInput").ap()
        dram["out"] = nc.dram_tensor("out_0", (D, S), F, kind="ExternalOutput").ap()
        dram["tab1"] = nc.dram_tensor("tab1", (8, P, L1), F).ap()
        dram["tab2"] = nc.dram_tensor("tab2", (8, P, L2), F).ap()
        dram["spill"] = nc.dram_tensor("spill", (D, S), F).ap()
        return dram

    plan = build(nc, scratch, mk)
    ins = {f"in_{k}": v for k, v in arrays.items()}
    ins["in_w"] = pack(plan, weight_table(a))
    r = _run(nc, [ins], core_ids=[0])
    return np.ascontiguousarray(r.results[0]["out_0"].T)[None]
```
